# Optimizing a Trainium2 kernel written in Bass

```python
import math
import jax, jax.numpy as jnp
from jax import lax
import numpy as np

D_MODEL = 1024
BATCH = 1
SEQ = 512
DEPTH = 1

D_CONV = 1024
CONV_K = 31
D_RNN = 1280
LRU_HEADS = 16
LRU_BLOCK = D_RNN // LRU_HEADS
LRU_CONV_K = 4
LRU_C = 8.0
D_FF = ((int(math.ceil(8 * D_MODEL / 3)) + 255) // 256) * 256
IN_SPLITS = (2 * D_CONV, D_RNN, D_RNN, D_MODEL, D_MODEL)
D_IN = sum(IN_SPLITS)
EPS = 1e-6


def rmsnorm(x, g):
    xf = x.astype(jnp.float32)
    y = xf * lax.rsqrt(jnp.mean(xf * xf, axis=-1, keepdims=True) + EPS)
    return (y * g.astype(jnp.float32)).astype(x.dtype)

def layernorm(x, g, b):
    xf = x.astype(jnp.float32)
    mu = jnp.mean(xf, axis=-1, keepdims=True)
    xc = xf - mu
    var = jnp.mean(xc * xc, axis=-1, keepdims=True)
    y = xc * lax.rsqrt(var + EPS) * g.astype(jnp.float32) + b.astype(jnp.float32)
    return y.astype(x.dtype)

def causal_depthwise_conv(u, w, b):
    k, c = w.shape
    u_pad = jnp.pad(u, ((0, 0), (k - 1, 0), (0, 0)))
    y = lax.conv_general_dilated(
        u_pad, w[:, None, :].astype(u.dtype), window_strides=(1,), padding='VALID',
        dimension_numbers=('NWC', 'WIO', 'NWC'), feature_group_count=c)
    return y + b.astype(u.dtype)

def _linear_recurrence_combine(left, right):
    a1, b1 = left
    a2, b2 = right
    return a1 * a2, a2 * b1 + b2

def rg_lru(xb, wa, ba, wx, bx, lam):
    bsz, s, d = xb.shape
    xf = xb.astype(jnp.float32)
    xh = xf.reshape(bsz, s, LRU_HEADS, LRU_BLOCK)
    r = jax.nn.sigmoid(jnp.einsum('bshi,hij->bshj', xh, wa.astype(jnp.float32)).reshape(bsz, s, d)
                       + ba.astype(jnp.float32))
    i = jax.nn.sigmoid(jnp.einsum('bshi,hij->bshj', xh, wx.astype(jnp.float32)).reshape(bsz, s, d)
                       + bx.astype(jnp.float32))
    log_a = -LRU_C * r * jax.nn.softplus(-lam.astype(jnp.float32))
    a = jnp.exp(log_a)
    mult = jnp.sqrt(-jnp.expm1(2.0 * log_a))
    bterm = mult * (i * xf)
    _, h = lax.associative_scan(_linear_recurrence_combine, (a, bterm), axis=1)
    return h.astype(xb.dtype)

def first_inputs(seed: int = 0) -> dict:
    key = jax.random.key(seed)
    ks = jax.random.split(key, 32)
    f32 = jnp.float32
    L = DEPTH

    def nrm(k, shape, fan_in, scale=1.0):
        return jax.random.normal(k, shape, f32) * (scale * fan_in ** -0.5)

    def small(k, shape, s=0.02):
        return jax.random.normal(k, shape, f32) * s

    x = jax.random.normal(ks[0], (BATCH, SEQ, D_MODEL), f32)
    a0 = jax.random.uniform(ks[16], (L, D_RNN), f32, 0.9, 0.999)
    lru_lambda = jnp.log(a0) - jnp.log1p(-a0)
    return {
        "x": x,
        "norm1_g": 1.0 + small(ks[1], (L, D_MODEL)),
        "w_in": nrm(ks[2], (L, D_MODEL, D_IN), D_MODEL),
        "b_in": small(ks[3], (L, D_IN)),
        "conv_dw_w": nrm(ks[4], (L, CONV_K, D_CONV), CONV_K),
        "conv_dw_b": small(ks[5], (L, D_CONV)),
        "conv_ln_g": 1.0 + small(ks[6], (L, D_CONV)),
        "conv_ln_b": small(ks[7], (L, D_CONV)),
        "conv_w_out": nrm(ks[8], (L, D_CONV, D_MODEL), D_CONV),
        "conv_b_out": small(ks[9], (L, D_MODEL)),
        "lru_conv_w": nrm(ks[10], (L, LRU_CONV_K, D_RNN), LRU_CONV_K),
        "lru_conv_b": small(ks[11], (L, D_RNN)),
        "lru_wa": nrm(ks[12], (L, LRU_HEADS, LRU_BLOCK, LRU_BLOCK), LRU_BLOCK),
        "lru_ba": small(ks[13], (L, D_RNN)),
        "lru_wx": nrm(ks[14], (L, LRU_HEADS, LRU_BLOCK, LRU_BLOCK), LRU_BLOCK),
        "lru_bx": small(ks[15], (L, D_RNN)),
        "lru_lambda": lru_lambda,
        "lru_w_out": nrm(ks[17], (L, D_RNN, D_MODEL), D_RNN),
        "w_mix_out": nrm(ks[18], (L, D_MODEL, D_MODEL), D_MODEL),
        "norm2_g": 1.0 + small(ks[19], (L, D_MODEL)),
        "ffn_w1": nrm(ks[20], (L, D_MODEL, D_FF), D_MODEL),
        "ffn_w3": nrm(ks[21], (L, D_MODEL, D_FF), D_MODEL),
        "ffn_w2": nrm(ks[22], (L, D_FF, D_MODEL), D_FF),
        "norm_f_g": 1.0 + small(ks[23], (D_MODEL,)),
    }

def first_block(x, norm1_g, w_in, b_in, conv_dw_w, conv_dw_b, conv_ln_g, conv_ln_b,
              conv_w_out, conv_b_out, lru_conv_w, lru_conv_b, lru_wa, lru_ba, lru_wx,
              lru_bx, lru_lambda, lru_w_out, w_mix_out, norm2_g, ffn_w1, ffn_w3, ffn_w2,
              norm_f_g):
    split_idx = list(np.cumsum(IN_SPLITS)[:-1])
    for l in range(DEPTH):
        h = rmsnorm(x, norm1_g[l])
        z = h @ w_in[l] + b_in[l]
        z_glu, z_rx, z_rg, z_ga, z_gb = jnp.split(z, split_idx, axis=-1)

        u = z_glu[..., :D_CONV] * jax.nn.sigmoid(z_glu[..., D_CONV:])
        u = causal_depthwise_conv(u, conv_dw_w[l], conv_dw_b[l])
        u = jax.nn.silu(layernorm(u, conv_ln_g[l], conv_ln_b[l]))
        y_a = u @ conv_w_out[l] + conv_b_out[l]

        xb = causal_depthwise_conv(z_rx, lru_conv_w[l], lru_conv_b[l])
        hb = rg_lru(xb, lru_wa[l], lru_ba[l], lru_wx[l], lru_bx[l], lru_lambda[l])
        y_b = (hb * jax.nn.gelu(z_rg, approximate=True)) @ lru_w_out[l]

        m = jax.nn.sigmoid(z_ga) * y_a + jax.nn.sigmoid(z_gb) * y_b
        x = x + m @ w_mix_out[l]

        h = rmsnorm(x, norm2_g[l])
        x = x + (jax.nn.silu(h @ ffn_w1[l]) * (h @ ffn_w3[l])) @ ffn_w2[l]
    return rmsnorm(x, norm_f_g)


D_FF_2 = 2816
N_MOD = 9
GLA_HEADS = 4
GLA_DK = D_MODEL // 2
GLA_DV = D_MODEL
GLA_HK = GLA_DK // GLA_HEADS
GLA_HV = GLA_DV // GLA_HEADS
GLA_RANK = 16
GLA_TAU = 16.0
GLA_CHUNK = 64
FOX_HEADS = 16
FOX_HD = D_MODEL // FOX_HEADS
FOX_W = FOX_HEADS * FOX_HD
Q_BLOCK = 128
SPLITS = (GLA_DK, GLA_DK, GLA_DV, GLA_RANK, GLA_DV, FOX_W, FOX_W, FOX_W, FOX_HEADS, D_MODEL, D_MODEL)
IN_COLS = 2 * GLA_DK + 2 * GLA_DV + GLA_RANK + 3 * FOX_W + FOX_HEADS + 2 * D_MODEL


def rmsnorm_2(x, g):
    xf = x.astype(jnp.float32)
    y = xf * lax.rsqrt(jnp.mean(xf * xf, axis=-1, keepdims=True) + EPS)
    return (y * g.astype(jnp.float32)).astype(x.dtype)

def swiglu(h, w_gu, w_dn):
    g, u = jnp.split(h @ w_gu, 2, axis=-1)
    return (jax.nn.silu(g) * u) @ w_dn

def gla_chunked(q, k, v, log_a):
    B, H, T, dk = q.shape
    dv = v.shape[-1]
    C = GLA_CHUNK
    N = T // C

    def to_chunks(a):
        return a.reshape(B, H, N, C, a.shape[-1]).transpose(2, 0, 1, 3, 4)

    qc, kc, vc, gc = to_chunks(q), to_chunks(k), to_chunks(v), to_chunks(log_a)
    causal = jnp.tril(jnp.ones((C, C), dtype=bool))[:, :, None]

    def step(S, inp):
        qi, ki, vi, gi = inp
        b = jnp.cumsum(gi, axis=2)
        o_inter = jnp.einsum('bhtd,bhde->bhte', qi * jnp.exp(b), S)
        diff = b[:, :, :, None, :] - b[:, :, None, :, :]
        decay = jnp.exp(jnp.where(causal, diff, -jnp.inf))
        A = jnp.einsum('bhtd,bhsd,bhtsd->bhts', qi, ki, decay)
        o = o_inter + jnp.einsum('bhts,bhse->bhte', A, vi)
        b_last = b[:, :, -1:, :]
        S_new = jnp.exp(b_last[:, :, 0, :, None]) * S + jnp.einsum(
            'bhsd,bhse->bhde', ki * jnp.exp(b_last - b), vi)
        return S_new, o

    S0 = jnp.zeros((B, H, dk, dv), jnp.float32)
    _, o = lax.scan(step, S0, (qc, kc, vc, gc))
    return o.transpose(1, 2, 0, 3, 4).reshape(B, H, T, dv)

def fox_attention(q, k, v, logf):
    B, H, T, hd = q.shape
    F = jnp.cumsum(logf, axis=-1)
    nb = T // Q_BLOCK
    qb = q.reshape(B, H, nb, Q_BLOCK, hd).transpose(2, 0, 1, 3, 4)
    Fb = F.reshape(B, H, nb, Q_BLOCK).transpose(2, 0, 1, 3)
    kpos = jnp.arange(T)
    scale = hd ** -0.5

    def block(args):
        qi, Fi, i = args
        s = jnp.einsum('bhqd,bhkd->bhqk', qi, k).astype(jnp.float32) * scale
        s = s + Fi[..., None] - F[:, :, None, :]
        qpos = i * Q_BLOCK + jnp.arange(Q_BLOCK)
        s = jnp.where(kpos[None, :] <= qpos[:, None], s, -jnp.inf)
        p = jax.nn.softmax(s, axis=-1)
        return jnp.einsum('bhqk,bhkd->bhqd', p.astype(v.dtype), v)

    o = lax.map(block, (qb, Fb, jnp.arange(nb)))
    return o.transpose(1, 2, 0, 3, 4).reshape(B, H, T, hd)

def token_mixer(h, w_in, w_a2, b_a, b_f, g_gla, w_pa, w_pb, w_out):
    B, T, _ = h.shape
    f32 = jnp.float32
    z = h @ w_in
    cuts = np.cumsum(SPLITS)[:-1].tolist()
    q_a, k_a, v_a, a_low, r_a, q_b, k_b, v_b, f_b, gate_a, gate_b = jnp.split(z, cuts, axis=-1)

    def heads(t, n):
        return t.reshape(B, T, n, -1).transpose(0, 2, 1, 3)

    log_a = jax.nn.log_sigmoid((a_low @ w_a2 + b_a).astype(f32)) / GLA_TAU
    o_a = gla_chunked(heads(q_a.astype(f32) * (GLA_HK ** -0.5), GLA_HEADS),
                      heads(k_a.astype(f32), GLA_HEADS),
                      heads(v_a.astype(f32), GLA_HEADS),
                      heads(log_a, GLA_HEADS))
    o_a = rmsnorm_2(o_a.transpose(0, 2, 1, 3), g_gla.reshape(GLA_HEADS, GLA_HV))
    o_a = o_a.astype(h.dtype).reshape(B, T, GLA_DV) * jax.nn.silu(r_a)

    logf = jax.nn.log_sigmoid((f_b + b_f).astype(f32)).transpose(0, 2, 1)
    o_b = fox_attention(heads(q_b, FOX_HEADS), heads(k_b, FOX_HEADS), heads(v_b, FOX_HEADS), logf)
    o_b = o_b.transpose(0, 2, 1, 3).reshape(B, T, FOX_W)

    merged = jax.nn.sigmoid(gate_a) * (o_a @ w_pa) + jax.nn.sigmoid(gate_b) * (o_b @ w_pb)
    return merged @ w_out

def second_inputs(seed: int = 0) -> dict:
    key = jax.random.key(seed)
    ks = jax.random.split(key, 20)
    L, D = DEPTH, D_MODEL
    nrm = jax.random.normal

    def w(k, shape, fan_in):
        return nrm(k, shape, jnp.float32) * fan_in ** -0.5

    return {
        "x": nrm(ks[0], (BATCH, SEQ, D), jnp.float32),
        "c": nrm(ks[1], (BATCH, D), jnp.float32),
        "w_ada": w(ks[2], (L, D, N_MOD * D), D) * 0.5,
        "b_ada": 0.02 * nrm(ks[3], (L, N_MOD * D), jnp.float32),
        "g_pre": 1.0 + 0.05 * nrm(ks[4], (L, 3, D), jnp.float32),
        "g_post": 1.0 + 0.05 * nrm(ks[5], (L, 3, D), jnp.float32),
        "w_gu1": w(ks[6], (L, D, 2 * D_FF_2), D),
        "w_dn1": w(ks[7], (L, D_FF_2, D), D_FF_2),
        "w_gu2": w(ks[8], (L, D, 2 * D_FF_2), D),
        "w_dn2": w(ks[9], (L, D_FF_2, D), D_FF_2),
        "w_in": w(ks[10], (L, D, IN_COLS), D),
        "w_a2": w(ks[11], (L, GLA_RANK, GLA_DK), GLA_RANK),
        "b_a": 0.1 * nrm(ks[12], (L, GLA_DK), jnp.float32),
        "b_f": 1.0 + 0.1 * nrm(ks[13], (L, FOX_HEADS), jnp.float32),
        "g_gla": 1.0 + 0.05 * nrm(ks[14], (L, GLA_DV), jnp.float32),
        "w_pa": w(ks[15], (L, GLA_DV, D), GLA_DV),
        "w_pb": w(ks[16], (L, FOX_W, D), FOX_W),
        "w_out": w(ks[17], (L, D, D), D),
    }

def second_block(x, c, w_ada, b_ada, g_pre, g_post, w_gu1, w_dn1, w_gu2, w_dn2,
              w_in, w_a2, b_a, b_f, g_gla, w_pa, w_pb, w_out):
    B = x.shape[0]
    for l in range(DEPTH):
        mods = (jax.nn.silu(c) @ w_ada[l] + b_ada[l]).reshape(B, N_MOD, 1, D_MODEL)
        sh1, sc1, gt1, sh2, sc2, gt2, sh3, sc3, gt3 = [mods[:, i] for i in range(N_MOD)]

        h = rmsnorm_2(x, g_pre[l, 0]) * (1 + sc1) + sh1
        x = x + 0.5 * gt1 * rmsnorm_2(swiglu(h, w_gu1[l], w_dn1[l]), g_post[l, 0])

        h = rmsnorm_2(x, g_pre[l, 1]) * (1 + sc2) + sh2
        y = token_mixer(h, w_in[l], w_a2[l], b_a[l], b_f[l], g_gla[l], w_pa[l], w_pb[l], w_out[l])
        x = x + gt2 * rmsnorm_2(y, g_post[l, 1])

        h = rmsnorm_2(x, g_pre[l, 2]) * (1 + sc3) + sh3
        x = x + 0.5 * gt3 * rmsnorm_2(swiglu(h, w_gu2[l], w_dn2[l]), g_post[l, 2])
    return x


def setup_inputs(seed=0):
    out = dict(first_inputs(seed))
    for name, value in second_inputs(seed + 1).items():
        if name != "x":
            out[name + "_2"] = value
    return out


def reference(
    x, norm1_g, w_in, b_in, conv_dw_w, conv_dw_b, conv_ln_g, conv_ln_b, conv_w_out, conv_b_out,
    lru_conv_w, lru_conv_b, lru_wa, lru_ba, lru_wx, lru_bx, lru_lambda, lru_w_out, w_mix_out,
    norm2_g, ffn_w1, ffn_w3, ffn_w2, norm_f_g, c_2, w_ada_2, b_ada_2, g_pre_2, g_post_2,
    w_gu1_2, w_dn1_2, w_gu2_2, w_dn2_2, w_in_2, w_a2_2, b_a_2, b_f_2, g_gla_2, w_pa_2, w_pb_2,
    w_out_2,
):
    x = first_block(
        x, norm1_g, w_in, b_in, conv_dw_w, conv_dw_b, conv_ln_g, conv_ln_b, conv_w_out,
        conv_b_out, lru_conv_w, lru_conv_b, lru_wa, lru_ba, lru_wx, lru_bx, lru_lambda,
        lru_w_out, w_mix_out, norm2_g, ffn_w1, ffn_w3, ffn_w2, norm_f_g,
    )
    return second_block(
        x, c_2, w_ada_2, b_ada_2, g_pre_2, g_post_2, w_gu1_2, w_dn1_2, w_gu2_2, w_dn2_2, w_in_2,
        w_a2_2, b_a_2, b_f_2, g_gla_2, w_pa_2, w_pb_2, w_out_2,
    )


_drawn_inputs = setup_inputs


def setup_inputs(seed=0):
    import zlib

    import numpy as np

    out = dict(_drawn_inputs(seed))
    spreads = {}
    factors = {'norm1_g': 4.742,
     'b_in': 2.683,
     'conv_dw_b': 10.443,
     'conv_ln_g': 28.54,
     'conv_ln_b': 29.64,
     'conv_b_out': 20.989,
     'lru_conv_b': 3.307,
     'lru_ba': 29.467,
     'lru_bx': 25.29,
     'norm2_g': 11.569,
     'norm_f_g': 2.668,
     'g_post_2': 3.064,
     'b_a_2': 4.912,
     'b_f_2': 52.408,
     'g_gla_2': 64.879,
     'w_pb_2': 4.3}
    for name, (base, spread) in spreads.items():
        noise = np.random.default_rng([zlib.crc32(name.encode()), seed]).standard_normal(out[name].shape)
        drawn = base * np.exp(spread * noise) if base else spread * noise
        out[name] = __import__('jax').numpy.asarray(drawn.astype(out[name].dtype))
    for name, factor in factors.items():
        out[name] = (out[name] * factor).astype(out[name].dtype)
    return out
```

```python
from contextlib import ExitStack

import concourse.bass as bass
from concourse import mybir

F32 = mybir.dt.float32
F32R = mybir.dt.float32r
I32 = mybir.dt.int32
U8 = mybir.dt.uint8
ACT = mybir.ActivationFunctionType
ALU = mybir.AluOpType
AX_X = mybir.AxisListType.X
ds = bass.ds

P = 128
T = 512
D = 1024
KD = D // P
D_RNN = 1280
KR = D_RNN // P
HEADS_LRU, LRU_BLOCK = 16, 80
TAPS, LTAPS = 31, 4
FF = 2816
FA, FB = 12, 10
PAD, LPAD = TAPS - 1, LTAPS - 1
EPS = 1e-6
GLA_HEADS, GLA_V = 4, 256
FOX_HEADS, FOX_HD = 16, 64
TAU = 16.0
RING, SRING, AHEAD = 8, 4, 3
SOME = 4 * P

UPTO = "all"


def k_panels(K, tiles):
    return -(-K * tiles // 4)


def make_plan():
    ffn = lambda n: [(f"gu{n}a", 4 * FA, 2 * FA), (f"dn{n}a", k_panels(FA, KD), KD),
                     (f"gu{n}b", 4 * FB, 2 * FB), (f"dn{n}b", k_panels(FB, KD), KD)]
    order = [("win", 104, 52), ("gates0", 10, 10), ("convo0", 8, 4), ("gates1", 10, 10), ("convo1", 8, 4),
             ("lruo", k_panels(KR, KD), KD), ("mix", 16, 8)] + ffn(1) + ffn(2)
    order += [("qka", 16, 8), ("va", 16, 8), ("low", 2, 0), ("rv", 32, 16), ("qkb", 64, 32),
              ("pa", 16, 8), ("pb", 16, 8), ("wout", 16, 8)] + ffn(3)
    plan, p, t = {}, 0, 0
    for name, panels, tiles in order:
        plan[name] = (p, t, panels, tiles)
        p += panels
        t += tiles
        if UPTO == "first" and name == "dn1b":
            break
        if UPTO == "ffn2" and name == "dn2b":
            break
    total = p
    if "qkb" in plan:
        p, t, panels, tiles = plan["qkb"]
        plan["gab"] = (p + 8, t + 4, panels, tiles)
    return plan, total


PER_TURN = {"qkb": (16, 2), "gab": (16, 2)}


def per_turn(name):
    return PER_TURN.get(name, (8, 1))


PLAN, NPANELS = make_plan()
X_FINAL = {"first": 0, "ffn2": 8, "all": 24}[UPTO]

COLS = {}
NCOLS = 0
for _n, _c in [("norm1_g", 8), ("b_in", 52), ("conv_dw_w", TAPS * 8), ("conv_dw_b", 8), ("conv_ln_g", 8),
               ("conv_ln_b", 8), ("conv_b_out", 8), ("lru_conv_w", LTAPS * 10), ("lru_conv_b", 10),
               ("lru_ba", 10), ("lru_bx", 10), ("lru_lambda", 10), ("norm2_g", 8), ("norm_f_g", 8),
               ("c_2", 8), ("b_ada_2", 72), ("g_pre_2", 24), ("g_post_2", 24), ("b_a_2", 4), ("g_gla_2", 8),
               ("b_f_2", 1)]:
    COLS[_n] = (NCOLS, _c)
    NCOLS += _c

FILL_A = {n: 8 * i for i, n in enumerate(["h1", "u2", "mix", "hf1", "hf2", "hmix2", "ob", "hf3"])}
FILL_B = {}
_b = 0
for _n, _c in [("xb", 10), ("yb", 10), ("ffn1a", FA), ("ffn1b", FB), ("ffn2a", FA), ("ffn2b", FB), ("oa", 8),
               ("merged", 8), ("ffn3a", FA), ("ffn3b", FB)]:
    FILL_B[_n] = _b
    _b += _c
NORM = {n: i for i, n in enumerate(["n1", "ln", "n2", "nf", "pre1", "post1", "pre2", "post2", "pre3", "post3"])}


GLA_IN = ["bc", "kc", "d1", "d2"]
for _l in range(1, 8):
    GLA_IN += [f"k{_l}", f"q{_l}"] + ([f"d{_l + 2}"] if _l < 6 else ["do"] if _l == 6 else [])
GLA_IN += [f"x{_n}" for _n in range(6)] + ["kd", "y"]
GLA_EXP = ["eb"]
for _l in range(1, 8):
    GLA_EXP += [f"ef{_l}", f"es{_l}"]
GLA_EXP += ["eo", "ao"] + [f"sq{_n}" for _n in range(4)] + [f"on{_n}" for _n in range(4)]
GLA_MM = [f"m{_l}" for _l in range(8)] + ["o0", "o1", "pv0", "pv1"]
GLA_CP = ["ms"] + [f"c{_l}" for _l in range(8)] + ["ao"]


def build(nc, stream, ada, xT, cols_d, consts_d, masks_d, wa2_d, out, spill_ga, spill_gb, spill_rv):
    ctx = ExitStack()
    with ctx:
        def sb(name, shape, dt=F32):
            return ctx.enter_context(nc.sbuf_tensor(name, shape, dt))

        def sem(name):
            return ctx.enter_context(nc.semaphore(name))

        raw = sb("raw", [P, RING, SOME])
        whi = sb("whi", [P, SRING, SOME], F32R)
        wlo = sb("wlo", [P, SRING, SOME], F32R)
        a_hi = sb("a_hi", [P, KD, T], F32R)
        a_lo = sb("a_lo", [P, KD, T], F32R)
        b_hi = sb("b_hi", [P, FA, T], F32R)
        b_lo = sb("b_lo", [P, FA, T], F32R)
        U_ST, X_ST = PAD + T, LPAD + T
        XR0 = (KD + 1) * U_ST
        X0 = XR0 + (KR + 1) * X_ST
        S0 = X0 + KR * T
        G_END = S0 + 9 * T
        G = sb("G", [P, G_END])
        sq = sb("sq", [P, 2, T])
        tmp = sb("tmp", [P, 2, T])
        cols = sb("cols", [P, NCOLS])
        consts = sb("consts", [P, 2, P])
        ones = sb("ones", [P, P])
        masks = sb("masks", [P, 8, P], U8)
        small = sb("small", [P, 8, 16])
        mods = sb("mods", [P, 72])
        derived = sb("derived", [P, 6, 8])
        lru_c = sb("lru_c", [P, 2, 10])
        lru_t = sb("lru_t", [P, 4, 10])
        epsc = sb("epsc", [P, 2])
        ident = consts[:, 0, :]
        tri = consts[:, 1, :]

        def col(name, k):
            at, n = COLS[name]
            return cols[:, at + k:at + k + 1] if isinstance(k, int) else cols[:, ds(k + at, 1)]

        def tiles(at, n):
            return G[:, at:at + n * T].rearrange("p (n t) -> p n t", t=T)

        X = tiles(X0, KD)
        U = G[:, 0:XR0].rearrange("p (n t) -> p n t", t=U_ST)
        XR = G[:, XR0:X0].rearrange("p (n t) -> p n t", t=X_ST)
        RG = tiles(X0, KR)
        R5 = tiles(S0, 5)
        IG = tiles(S0 + 5 * T, 2)
        AR = tiles(S0 + 7 * T, 2)
        STG = tiles(S0, 2)
        GA = tiles(0, KD)
        GB = tiles(XR0, KD)
        Y = tiles(0, KD)
        A5 = [AR[:, 0, :], AR[:, 1, :], G[:, KD * T:(KD + 1) * T], sq[:, 0, :], sq[:, 1, :]]
        ADA = G[:, KD * T:KD * T + 2 * D].rearrange("p (n t) -> p n t", t=D)
        ADA_ACC = G[:, KD * T + 2 * D:KD * T + 3 * D]
        SIL = tiles(KD * T + 3 * D, 2)
        QK = tiles(0, 8)
        LA = tiles(8 * T, 4)
        VA = G[:, 12 * T:20 * T].rearrange("p (n t) -> p n t", t=D)
        B0 = X0 + KD * T
        BC, KC, EE, EB, KQ, AD = (G[:, B0 + i * T:B0 + (i + 1) * T] for i in range(6))
        QX = G[:, B0 + 6 * T:B0 + 6 * T + 6 * P]
        AO = G[:, B0 + 6 * T + 6 * P:B0 + 6 * T + 12 * P]
        ON = G[:, B0 + 9 * T:B0 + 11 * T].rearrange("p (n t) -> p n t", t=GLA_V)
        LT = tiles(B0, 5)
        wa2 = G[0:16, B0 + 5 * T:B0 + 6 * T]
        RESET, LOW = sq[:, 0, :], sq[:, 1, :]
        E2 = [KC, EE]
        ONH = G[:, 0:8 * T].rearrange("p (h t e) -> p h t e", h=GLA_HEADS, e=GLA_V)
        R2 = G[:, B0:B0 + 8 * T].rearrange("p (n t) -> p n t", t=D)
        VB = VA
        OB = G[:, 0:8 * T].rearrange("p (n t) -> p n t", t=D)
        QF = tiles(8 * T, 4)
        STG2 = tiles(B0 + 6 * T, 2)
        PR, PT, NFH = tiles(B0, 2), tiles(B0 + 2 * T, 2), tiles(B0 + 4 * T, 2)
        GA2, GB2 = tiles(12 * T, KD), tiles(B0, KD)
        assert B0 + 11 * T <= G_END and 20 * T <= X0

        bank = [ctx.enter_context(nc.psum_tensor(f"bank{i}", [P, T], F32)) for i in range(8)]
        AUX, BCAST = bank[4], bank[5]

        raw_landed = [sem(f"raw_landed{i}") for i in range(RING)]
        hi_done = sem("hi_done")
        lo_done = sem("lo_done")
        used = sem("used")
        evac = [sem(f"evac{i}") for i in range(4)]
        a_val, a_hi_w, opa = sem("a_val"), sem("a_hi_w"), sem("opa")
        b_val, b_hi_w, opb = sem("b_val"), sem("b_hi_w"), sem("opb")
        ld_x, ld_c, ld_w2, ld_ga, ld_gb, ld_x2 = (sem(n) for n in ("ld_x", "ld_c", "ld_w2", "ld_ga", "ld_gb", "ld_x2"))
        vchain = sem("vchain")
        achain = sem("achain")
        const_ready = sem("const_ready")
        sq_ready = sem("sq_ready")
        sq_summed = sem("sq_summed")
        mean_summed = sem("mean_summed")
        st_ready = sem("st_ready")
        bc_ready = sem("bc_ready")
        x_ready = sem("x_ready")
        stage_full = sem("stage_full")
        stage_out = [sem("stage_out0"), sem("stage_out1")]
        conv_done = sem("conv_done")
        centred = sem("centred")
        u_silu = sem("u_silu")
        ix_done = sem("ix_done")
        decay = sem("decay")
        var_ready = sem("var_ready")
        root = sem("root")
        lru_done = sem("lru_done")
        lam_e, silc = sem("lam_e"), sem("silc")
        ada_landed = [sem("ada_landed0"), sem("ada_landed1")]
        ada_used = sem("ada_used")
        ada_psum = sem("ada_psum")
        out_done = sem("out_done")
        low_out, low_ready = sem("low_out"), sem("low_ready")
        la_psum, la_z, la_ln, la_done = sem("la_psum"), sem("la_z"), sem("la_ln"), sem("la_done")
        gla_in = sem("gla_in")
        gla_exp = sem("gla_exp")
        gla_mm = sem("gla_mm")
        gla_cp = sem("gla_cp")
        fox_nf, fox_s, fox_m, fox_p, fox_t, fox_pt, fox_o, fox_out = (
            sem(f"fox_{n}") for n in ("nf", "s", "m", "p", "t", "pt", "o", "out"))
        ob_t = sem("ob_t")
        rows_out = [sem("rows_out0"), sem("rows_out1")]
        gate2 = sem("gate2")
        oa_t, r_silu, r_prod, ld_r, ld_v = sem("oa_t"), sem("r_silu"), sem("r_prod"), sem("ld_r"), sem("ld_v")

        class Steps:
            def __init__(self, eng, s):
                self.eng, self.s, self.n, self.i, self.per = eng, s, 0, None, 0

            def next(self, ins):
                self.n += 1
                ins.then_inc(self.s, 1)
                self.eng.wait_ge(self.s, self.n if self.i is None else self.i * self.per + self.n)

            def begin(self, i, per):
                self.i, self.per, self.at = i, per, self.n

            def end(self, turns):
                assert self.n - self.at == self.per, (self.n - self.at, self.per)
                self.n += self.per * (turns - 1)
                self.i = None

        def wait_used(eng, name, i, s):
            eng.wait_ge(used, i * per_turn(name)[0] + (PLAN[name][0] + s + 1 + SRING))

        def wait_evac(eng, name, i, j):
            t = PLAN[name][1] + j
            eng.wait_ge(evac[t % 4], i * per_turn(name)[1] + (t // 4 + 2))

        def bank_of(name, j):
            return bank[(PLAN[name][1] + j) % 4]

        def evac_of(name, j):
            return evac[(PLAN[name][1] + j) % 4]

        block = ctx.enter_context(nc.Block())

        @block.sync
        def _(sp):
            def load(base, i, s):
                p = base + s
                sp.wait_ge(lo_done, i * 8 + (p + 1))
                src = stream[p] if isinstance(i, int) else stream[ds(i * 8 + p, 1)].rearrange("a p c -> p (a c)")
                sp.dma_start(raw[:, p % RING, :], src).then_inc(raw_landed[p % RING], 16)

            def load_run(base, n):
                whole = n // 8 * 8 if n >= 16 else 0
                if whole:
                    with sp.Fori(0, whole // 8) as i:
                        for s in range(8):
                            load(base, i, s)
                for s in range(whole, n):
                    load(base + s, 0, 0)

            def ada_run(gu, mod0, turns):
                base = PLAN[gu][0] + 8
                with sp.Fori(0, turns) as i:
                    for s in range(8):
                        load(base, i, s)
                        if s == 0 and mod0 == 0:
                            sp.wait_ge(used, PLAN[gu][0] + 1 + SRING)
                        sp.wait_ge(ada_used, i * 8 + (8 * mod0 + s + 1))
                        sp.dma_start(ADA[:, s % 2, :], ada[ds(i * 8 + (8 * mod0 + s), 1)].rearrange(
                            "a p c -> p (a c)")).then_inc(ada_landed[s % 2], 16)

            if UPTO == "first":
                load_run(0, NPANELS)
            else:
                a, b = PLAN["gu1a"][0] + 8, PLAN["gu1b"][0] + 8
                load_run(0, a)
                ada_run("gu1a", 0, 6)
                load_run(a + 48, b - a - 48)
                ada_run("gu1b", 6, 3)
                load_run(b + 24, NPANELS - b - 24)
            for k in range(KD):
                sp.wait_ge(x_ready, X_FINAL + k + 1)
                sp.dma_start(out[:, k, :], X[:, k, :]).then_inc(out_done, 16)
            sp.wait_ge(out_done, 16 * KD)

        @block.gpsimd
        def _(pool):
            def low(i, s):
                pool.wait_ge(hi_done, i * 8 + (s + 1))
                pool.tensor_tensor(wlo[:, s % SRING, :], raw[:, s % RING, :], whi[:, s % SRING, :].bitcast(F32),
                                   ALU.subtract).then_inc(lo_done, 1)

            pool.wait_ge(const_ready, 1)
            with pool.Fori(0, NPANELS // 8) as i:
                for s in range(8):
                    low(i, s)
            for s in range(NPANELS // 8 * 8, NPANELS):
                low(0, s)

        @block.scalar
        def _(act):
            own = Steps(act, achain)

            def split(name, i, s):
                p = PLAN[name][0] + s
                if isinstance(i, int) and p + 8 * i >= NPANELS:
                    return
                n = per_turn(name)[0]
                act.wait_ge(raw_landed[p % RING], i * (16 * n // RING) + (p // RING + 1) * 16)
                act.wait_ge(used, i * n + (p + 1))
                act.activation(whi[:, p % SRING, :], raw[:, p % RING, :], ACT.Copy).then_inc(hi_done, 1)

            def tick(name, i, s, n=2):
                for x in range(s, s + n):
                    split(name, i, x + AHEAD)

            def square(norm, k, value):
                if 8 * norm + k - 1 > 0:
                    act.wait_ge(sq_summed, 8 * norm + k - 1)
                act.activation(sq[:, k % 2, :], value, ACT.Square).then_inc(sq_ready, 1)

            def round_a(fill, val, shift=None):
                for k in range(KD):
                    act.wait_ge(a_val, val + k + 1)
                    if shift is None:
                        act.activation(a_hi[:, k, :], tmp[:, k % 2, :], ACT.Copy).then_inc(a_hi_w, 1)
                    else:
                        act.activation(a_hi[:, k, :], tmp[:, k % 2, :], ACT.Identity, bias=shift(k)).then_inc(a_hi_w, 1)

            def packed_tick(name, m, K):
                lo, hi = -(-m * K // 4), -(-(m + 1) * K // 4)
                tick(name, 0, lo, hi - lo)

            def ffn_gates(name, turns):
                with act.Fori(0, turns) as i:
                    for pr in range(2):
                        tick(name, i, 4 * pr)
                        wait_used(act, name, i, 4 * pr + 1)
                        wait_evac(act, name, i, 2 * pr + 1 - 4)
                        act.activation(SIL[:, pr, :], bank_of(name, 2 * pr)[:, :], ACT.Silu)\
                           .then_inc(evac_of(name, 2 * pr), 1)
                        tick(name, i, 4 * pr + 2)
                        wait_evac(act, name, i, 2 * pr + 1)
                        act.activation(b_hi[:, ds(i * 2 + pr, 1), :].rearrange("p a t -> p (a t)"), tmp[:, pr, :],
                                       ACT.Copy).then_inc(b_hi_w, 1)

            def ffn_down(name, K, norm, copy):
                for m in range(KD):
                    packed_tick(name, m, K)
                    if copy:
                        wait_used(act, name, 0, ((m + 1) * K - 1) // 4)
                        act.activation(Y[:, m, :], bank_of(name, m)[:, :], ACT.Copy).then_inc(evac_of(name, m), 1)
                    if norm is not None:
                        wait_evac(act, name, 0, m)
                        square(norm, m, (X if norm in (NORM["n2"], NORM["nf"]) else Y)[:, m, :])

            def ffn(n, norm):
                ffn_gates(f"gu{n}a", FA // 2)
                ffn_down(f"dn{n}a", FA, None, n > 1)
                ffn_gates(f"gu{n}b", FB // 2)
                ffn_down(f"dn{n}b", FB, norm, False)

            act.dma_start(cols[:, :], cols_d).then_inc(ld_c, 16)
            act.dma_start(consts[:, :, :], consts_d).then_inc(ld_c, 16)
            act.dma_start(G[:, S0:S0 + 8 * P], masks_d.rearrange("p a b -> p (a b)")).then_inc(ld_c, 16)
            act.dma_start(X[:, :, :], xT).then_inc(ld_x, 16)
            act.wait_ge(const_ready, 1)
            for s in range(AHEAD):
                split("win", 0, s)
            act.wait_ge(ld_x, 16)
            for k in range(KD):
                square(NORM["n1"], k, X[:, k, :])
            act.wait_ge(ld_c, 48)
            own.next(act.activation(lru_t[:, 0, :], cols[:, COLS["lru_lambda"][0]:COLS["lru_lambda"][0] + KR], ACT.Abs))
            act.activation(lru_t[:, 1, :], lru_t[:, 0, :], ACT.Exp, scale=-1.0).then_inc(lam_e, 1)
            act.activation(small[:, 7, 0:8], cols[:, COLS["c_2"][0]:COLS["c_2"][0] + 8], ACT.Silu).then_inc(silc, 1)
            round_a("h1", 0)

            with act.Fori(0, 4) as i:
                for pr in range(2):
                    tick("win", i, 4 * pr, 4)
                    wait_used(act, "win", i, 4 * pr + 3)
                    wait_evac(act, "win", i, 2 * pr - 4)
                    act.activation(R5[:, pr, :], bank[2 * pr + 1][:, :], ACT.Sigmoid,
                                   bias=cols[:, ds(i * 4 + (COLS["b_in"][0] + 2 * pr + 1), 1)])\
                       .then_inc(evac[2 * pr + 1], 1)
            for t in range(16, 16 + 2 * KR):
                m = (t - 16) % KR
                tick("win", 0, 2 * t)
                wait_used(act, "win", 0, 2 * t + 1)
                act.activation(XR[:, m + 1, LPAD:X_ST] if t < 16 + KR else RG[:, m, :], bank[t % 4][:, :],
                               ACT.Identity if t < 16 + KR else ACT.Gelu_apprx_tanh, bias=col("b_in", t))\
                   .then_inc(evac[t % 4], 1)
            wait_evac(act, "win", 0, 12)
            wait_evac(act, "win", 0, 14)
            for m in range(2 * KD):
                t = 16 + 2 * KR + m
                tick("win", 0, 2 * t)
                wait_used(act, "win", 0, 2 * t + 1)
                if m >= 2:
                    act.wait_ge(stage_out[m % 2], 16 * (m // 2))
                act.activation(STG[:, m % 2, :], bank[t % 4][:, :], ACT.Sigmoid, bias=col("b_in", t))\
                   .then_inc(evac[t % 4], 1)
                wait_evac(act, "win", 0, t)
                act.dma_start((spill_ga if m < KD else spill_gb)[:, m % KD, :], STG[:, m % 2, :])\
                   .then_inc(stage_out[m % 2], 16)
            for j in range(2):
                act.wait_ge(stage_out[j], 16 * KD)

            def lru_gates(half):
                name = f"gates{half}"
                for m in range(5):
                    if half:
                        act.wait_ge(lru_done, m + 1)
                    for w in range(2):
                        o = 2 * m + w
                        tick(name, 0, o, 1)
                        wait_used(act, name, 0, o)
                        n = 5 * half + m
                        if w and n >= 2:
                            act.wait_ge(ix_done, n - 1)
                        act.activation(R5[:, m, :] if w == 0 else IG[:, n % 2, :], bank_of(name, o)[:, :], ACT.Sigmoid,
                                       bias=col("lru_bx" if w else "lru_ba", n)).then_inc(evac_of(name, o), 1)

            def lru_decay(half):
                for m in range(5):
                    n = 5 * half + m
                    wait_evac(act, f"gates{half}", 0, 2 * m)
                    act.activation(A5[m], R5[:, m, :], ACT.Exp, scale=lru_c[:, 0, n:n + 1]).then_inc(achain, 1)
                    own.n += 1
                    act.wait_ge(achain, own.n)
                    act.activation(R5[:, m, :], R5[:, m, :], ACT.Tanh, scale=lru_c[:, 1, n:n + 1]).then_inc(decay, 1)

            def lru_root(half):
                for m in range(5):
                    act.wait_ge(var_ready, 5 * half + m + 1)
                    act.activation(R5[:, m, :], R5[:, m, :], ACT.Sqrt).then_inc(root, 1)

            lru_gates(0)
            for k in range(KD):
                act.wait_ge(centred, k + 1)
                square(NORM["ln"], k, U[:, k, PAD:U_ST])
            for k in range(KD):
                act.wait_ge(a_val, 8 + k + 1)
                act.activation(tmp[:, k % 2, :], tmp[:, k % 2, :], ACT.Silu, bias=col("conv_ln_b", k)).then_inc(u_silu, 1)
            act.dma_start(GA[:, :, :], spill_ga).then_inc(ld_ga, 16)
            lru_decay(0)
            for m in range(4):
                tick("convo0", 0, 2 * m)
            lru_root(0)
            lru_gates(1)
            lru_decay(1)
            tick("convo1", 0, 0)
            tick("convo1", 0, 2)
            lru_root(1)
            tick("convo1", 0, 4)
            tick("convo1", 0, 6)
            act.wait_ge(opb, FILL_B["yb"] + KR)
            act.dma_start(GB[:, :, :], spill_gb).then_inc(ld_gb, 16)
            act.dma_start(X[:, :, :], xT).then_inc(ld_x2, 16)
            for m in range(KD):
                packed_tick("lruo", m, KR)
                act.wait_ge(a_val, 16 + m + 1)
                act.activation(a_hi[:, m, :], tmp[:, m % 2, :], ACT.Copy).then_inc(a_hi_w, 1)
            for m in range(KD):
                tick("mix", 0, 2 * m)
                wait_evac(act, "mix", 0, m)
                square(NORM["n2"], m, X[:, m, :])
            round_a("hf1", 24)
            ffn(1, NORM["nf"])
            if UPTO == "first":
                return
            for k in range(KD):
                act.wait_ge(x_ready, k + 1)
                square(NORM["pre1"], k, X[:, k, :])
            round_a("hf2", 32, lambda k: mods[:, k:k + 1])
            ffn(2, NORM["post1"])
            for k in range(KD):
                act.wait_ge(x_ready, KD + k + 1)
                if UPTO != "ffn2":
                    square(NORM["pre2"], k, X[:, k, :])
            if UPTO == "ffn2":
                return

            def rows_tick(name, i):
                tick(name, i, 0, 8)
                wait_used(act, name, i, 7)

            round_a("hmix2", 40, lambda k: mods[:, 24 + k:25 + k])
            for t in range(8):
                tick("qka", 0, 2 * t)
                wait_used(act, "qka", 0, 2 * t + 1)
                act.activation(QK[:, t % 4 * 2 + t // 4, :], bank_of("qka", t)[:, :], ACT.Copy,
                               scale=float(P) ** -0.5 if t < 4 else 1.0).then_inc(evac_of("qka", t), 1)
            for i in range(2):
                rows_tick("va", i)
                for t in range(4):
                    act.activation(VA[:, t, i * SOME:(i + 1) * SOME], bank_of("va", t)[:, :], ACT.Copy)\
                       .then_inc(evac_of("va", t), 1)
            act.dma_start(wa2, wa2_d).then_inc(ld_w2, 16)
            tick("low", 0, 0)
            wait_used(act, "low", 0, 1)
            act.activation(LOW[0:16, :], AUX[0:16, :], ACT.Copy).then_inc(low_out, 1)
            act.activation(LOW[32:48, :], AUX[32:48, :], ACT.Identity, bias=cols[32:48, COLS["b_f_2"][0]:NCOLS])\
               .then_inc(low_out, 1)
            for h in range(GLA_HEADS):
                act.wait_ge(la_psum, h + 1)
                act.activation(LA[:, h, :], bank[6 + h % 2][:, :], ACT.Identity, bias=col("b_a_2", h)).then_inc(la_z, 1)
            act.wait_ge(la_z, GLA_HEADS)
            act.wait_ge(low_out, 2)
            for func, scale, bias in ((ACT.Abs, 1.0, 0.0), (ACT.Exp, -1.0, 0.0), (ACT.Ln, 1.0, 1.0)):
                for h in range(5):
                    rows = slice(0, P) if h < 4 else slice(32, 48)
                    src = LT[rows, h, :] if func != ACT.Abs else (LA[rows, h, :] if h < 4 else LOW[rows, :])
                    if func == ACT.Ln:
                        act.activation(LT[rows, h, :], src, func, scale=scale, bias=bias).then_inc(la_ln, 1)
                    else:
                        own.next(act.activation(LT[rows, h, :], src, func, scale=scale))

            with act.Fori(0, GLA_HEADS) as i:
                def wait_in(what):
                    act.wait_ge(gla_in, i * len(GLA_IN) + (GLA_IN.index(what) + 2))

                def wait_mm(what):
                    act.wait_ge(gla_mm, i * len(GLA_MM) + (GLA_MM.index(what) + 2))

                def keep_rows(t):
                    if t == 0:
                        wait_used(act, "rv", i, 7)
                    act.wait_ge(rows_out[t % 2], i * 32 + 16 * (t // 2 + 1))
                    act.activation(tmp[:, t % 2, :], bank_of("rv", t)[:, :], ACT.Copy).then_inc(evac_of("rv", t), 1)
                    wait_evac(act, "rv", i, t)
                    act.dma_start(spill_rv[:, ds(i * 4 + t, 1), :].rearrange("p a t -> p (a t)"), tmp[:, t % 2, :])\
                       .then_inc(rows_out[t % 2], 16)

                for label in GLA_EXP:
                    kind, arg = label[:2], int(label[2:] or 0)
                    if kind == "eb":
                        wait_in("bc")
                        ins = act.activation(EB, BC, ACT.Exp, scale=1 / TAU)
                        tick("rv", i, 0, 1)
                    elif kind in ("ef", "es"):
                        if kind == "ef":
                            tick("rv", i, arg, 1)
                        wait_in(f"d{arg}")
                        m = P >> arg
                        half = slice(0, m) if kind == "ef" else slice(m, 2 * m)
                        v = E2[arg % 2].rearrange("p (n m) -> p n m", m=2 * m)[:, :, half]
                        ins = act.activation(v, v, ACT.Exp, scale=-1 / TAU if kind == "ef" else 1 / TAU)
                    elif kind == "eo":
                        wait_in("do")
                        ins = act.activation(E2[0], E2[0], ACT.Exp, scale=1 / TAU)
                    elif kind == "ao":
                        wait_mm("o1")
                        ins = act.activation(AO[:, 3 * P:6 * P], bank[7][:, 0:3 * P], ACT.Copy)
                    else:
                        out_ps = bank[4 + arg // 2][:, arg % 2 * GLA_V:(arg % 2 + 1) * GLA_V]
                        if kind == "sq":
                            if arg == 0:
                                keep_rows(0)
                                keep_rows(1)
                            wait_mm(f"pv{arg // 2}")
                            ins = act.activation(ON[:, arg, :], out_ps, ACT.Square, accum_out=small[:, 5, arg:arg + 1])
                        else:
                            if arg == 0:
                                keep_rows(2)
                                keep_rows(3)
                            wait_in("y")
                            ins = act.activation(ONH[:, ds(i, 1), arg, :].rearrange("p a e -> p (a e)"), out_ps, ACT.Copy,
                                                 scale=small[:, 6, arg:arg + 1])
                    ins.then_inc(gla_exp, 1)
            for j in range(2):
                act.wait_ge(rows_out[j], 16 * (2 * GLA_HEADS + 1))
            for dst, at, landed in ((R2, 0, ld_r), (VB, 8, ld_v)):
                for g in range(2):
                    act.dma_start(dst[:, :, g * SOME:(g + 1) * SOME], spill_rv[:, at + 4 * g:at + 4 * g + 4, :])\
                       .then_inc(landed, 16)
            act.wait_ge(ld_r, 32)
            for t in range(4):
                act.activation(R2[:, t, :], R2[:, t, :], ACT.Silu).then_inc(r_silu, 1)
            for m in range(KD):
                act.wait_ge(b_val, m + 1)
                act.activation(b_hi[:, m, :], tmp[:, m % 2, :], ACT.Copy).then_inc(b_hi_w, 1)

            with act.Fori(0, FOX_HEADS // 4) as i:
                for j in range(4):
                    tick("qkb", i, 2 * j)
                    wait_used(act, "qkb", i, 2 * j + 1)
                    act.activation(QF[:, j, :], bank_of("qkb", j)[:, :], ACT.Copy,
                                   scale=FOX_HD ** -0.5 if j % 2 == 0 else 1.0).then_inc(evac_of("qkb", j), 1)
                for u in range(17):
                    if u < 16:
                        n = (u % 4 + 1) * P
                        act.wait_ge(fox_m, i * 16 + (u + 1))
                        act.wait_ge(fox_t, i * 16 + (u + 1))
                        act.activation(PR[:, u % 2, 0:n], bank[6 + u % 2][:, 0:n], ACT.Exp,
                                       bias=small[:, 6, u % 4:u % 4 + 1], accum_out=small[:, 5, u % 4:u % 4 + 1])\
                           .then_inc(fox_p, 1)
                        if u % 2 == 0:
                            tick("gab", i, u // 2, 1)
                    if u:
                        w = u - 1
                        n = (w % 4 + 1) * P
                        act.wait_ge(fox_t, i * 16 + (w + 3))
                        act.wait_ge(fox_o, i * 16 + (w + 1))
                        act.activation(PT[:, w % 2, 0:n], bank[4 + w % 2][:, 0:n], ACT.Copy).then_inc(fox_pt, 1)
                        if w % 4 == 3:
                            j = w // 4
                            wait_used(act, "gab", i, 2 * j + 1)
                            act.wait_ge(stage_out[j % 2], i * 32 + 16 * (KD + j // 2))
                            act.activation(STG2[:, j % 2, :], bank_of("gab", j)[:, :], ACT.Copy)\
                               .then_inc(evac_of("gab", j), 1)
                            wait_evac(act, "gab", i, j)
                            act.dma_start(spill_rv[:, ds(i * 4 + j, 1), :].rearrange("p a t -> p (a t)"),
                                          STG2[:, j % 2, :]).then_inc(stage_out[j % 2], 16)
            for j in range(2):
                act.wait_ge(stage_out[j], 16 * 2 * KD)
            act.wait_ge(fox_o, 4 * FOX_HEADS + 2)
            act.dma_start(GA2[:, :, :], spill_rv[:, 0:KD, :]).then_inc(ld_ga, 16)
            act.dma_start(GB2[:, :, :], spill_rv[:, KD:2 * KD, :]).then_inc(ld_gb, 16)
            for m in range(KD):
                act.wait_ge(ob_t, m + 1)
                act.activation(a_hi[:, m, :], bank[6 + m % 2][:, :], ACT.Copy).then_inc(a_hi_w, 1)
            act.wait_ge(ld_ga, 32)
            for m in range(KD):
                tick("pa", 0, 2 * m)
                act.activation(GA2[:, m, :], GA2[:, m, :], ACT.Sigmoid).then_inc(gate2, 1)
            act.wait_ge(ld_gb, 32)
            for m in range(KD):
                act.activation(GB2[:, m, :], GB2[:, m, :], ACT.Sigmoid).then_inc(gate2, 1)
            for m in range(KD):
                tick("pb", 0, 2 * m)
                act.wait_ge(b_val, KD + m + 1)
                act.activation(b_hi[:, m, :], tmp[:, m % 2, :], ACT.Copy).then_inc(b_hi_w, 1)
            for m in range(KD):
                tick("wout", 0, 2 * m)
                wait_used(act, "wout", 0, 2 * m + 1)
                act.activation(Y[:, m, :], bank_of("wout", m)[:, :], ACT.Copy).then_inc(evac_of("wout", m), 1)
                wait_evac(act, "wout", 0, m)
                square(NORM["post2"], m, Y[:, m, :])
            for k in range(KD):
                act.wait_ge(x_ready, 2 * KD + k + 1)
                square(NORM["pre3"], k, X[:, k, :])
            round_a("hf3", 48, lambda k: mods[:, 48 + k:49 + k])
            ffn(3, NORM["post3"])

        @block.tensor
        def _(pe):
            def panel(name, i, s, ks, out_ps, ops, first, last, q0=0, done=True):
                p = PLAN[name][0] + s
                pe.wait_ge(lo_done, i * per_turn(name)[0] + (p + 1 + RING))
                hi, lo = ops
                for q, k in enumerate(ks):
                    c = slice((q0 + q) * P, (q0 + q + 1) * P)
                    w_hi, w_lo = whi[:, p % SRING, c], wlo[:, p % SRING, c]
                    pe.matmul(out_ps, w_hi, hi[:, k, :], start=first and q == 0, stop=False)
                    pe.matmul(out_ps, w_lo, hi[:, k, :], start=False, stop=False)
                    mm = pe.matmul(out_ps, w_hi, lo[:, k, :], start=False, stop=last and q == len(ks) - 1)
                if done:
                    mm.then_inc(used, 1)

            def bank_free(name, i, j):
                t = PLAN[name][1] + j
                pe.wait_ge(evac[t % 4], i * per_turn(name)[1] + (t // 4 + 1))

            OPA, OPB = (a_hi, a_lo), (b_hi, b_lo)

            def tile8(name, i, j, ops, ready, fill, wait_ops):
                bank_free(name, i, j)
                for h in range(2):
                    if wait_ops:
                        pe.wait_ge(ready, fill + 4 * h + 4)
                    panel(name, i, 2 * j + h, range(4 * h, 4 * h + 4), bank_of(name, j)[:, :], ops, h == 0, h == 1)

            def stage8(name, ops, ready, fill, turns):
                with pe.Fori(0, turns) as i:
                    for j in range(4):
                        tile8(name, i, j, ops, ready, fill, j == 0)

            def tile_packed(name, m, K, ops, ready, fill):
                bank_free(name, 0, m)
                k = 0
                while k < K:
                    f = m * K + k
                    n = min(4 - f % 4, K - k)
                    if m == 0:
                        pe.wait_ge(ready, fill + k + n)
                    panel(name, 0, f // 4, range(k, k + n), bank_of(name, m)[:, :], ops, k == 0, k + n == K,
                          q0=f % 4, done=(f + n) % 4 == 0)
                    k += n

            def sum_tile(k, value, done):
                for tt in range(4):
                    mm = pe.matmul(AUX[:, tt:tt + 1], value[:, tt * P:(tt + 1) * P], ones[:, 0:1],
                                   start=(k == 0 and tt == 0), stop=(k == KD - 1 and tt == 3), skip_group_check=True)
                mm.then_inc(done, 1)

            def sum_square(norm, k):
                pe.wait_ge(sq_ready, 8 * norm + k + 1)
                sum_tile(k, sq[:, k % 2, :], sq_summed)

            def broadcast(n):
                pe.wait_ge(st_ready, n)
                pe.matmul(BCAST[:, :], ones[:, :], tmp[:, 0, :], start=True, stop=True).then_inc(bc_ready, 1)

            def ffn(n, norm, ada_mods, fill):
                for half, K in (("a", FA), ("b", FB)):
                    name = f"gu{n}{half}"
                    turns = K // 2
                    with_ada = 0 if not ada_mods else (6 if half == "a" else 3)
                    if with_ada:
                        with pe.Fori(0, with_ada) as i:
                            for j in range(4):
                                tile8(name, i, j, OPA, opa, fill, j == 0)
                            m0 = 0 if half == "a" else 6
                            pe.wait_ge(ada_used, i * 8 + (8 * m0 + 8 + 2))
                            for j in range(8):
                                mm = pe.matmul(AUX[:, 8 + j:9 + j], ADA_ACC[:, j * P:(j + 1) * P], ones[:, 0:1],
                                               start=(j == 0), stop=(j == 7), skip_group_check=True)
                            mm.then_inc(ada_psum, 1)
                    if turns > with_ada:
                        with pe.Fori(with_ada, turns) as i:
                            for j in range(4):
                                tile8(name, i, j, OPA, opa, fill, j == 0)
                    name = f"dn{n}{half}"
                    for m in range(KD):
                        tile_packed(name, m, K, OPB, opb, FILL_B[f"ffn{n}{half}"])
                        if half == "b" and m:
                            sum_square(norm, m - 1)
                sum_square(norm, KD - 1)

            pe.wait_ge(const_ready, 1)
            for k in range(KD):
                sum_square(NORM["n1"], k)
            broadcast(1)
            stage8("win", OPA, opa, FILL_A["h1"], 13)
            for k in range(KD):
                pe.wait_ge(conv_done, k + 1)
                sum_tile(k, U[:, k, PAD:U_ST], mean_summed)
            broadcast(2)

            def lru_gates(half):
                name = f"gates{half}"
                for o in range(10):
                    m = o // 2
                    ks = [k for k in (m - 1, m, m + 1) if 0 <= k < 5]
                    bank_free(name, 0, o)
                    pe.wait_ge(opb, FILL_B["xb"] + 5 * half + ks[-1] + 1)
                    panel(name, 0, o, [5 * half + k for k in ks], bank_of(name, o)[:, :], OPB, True, True,
                          q0=ks[0] - m + 1)

            lru_gates(0)
            for k in range(KD):
                sum_square(NORM["ln"], k)
            broadcast(3)
            for m in range(4):
                tile8("convo0", 0, m, OPA, opa, FILL_A["u2"], m == 0)
            lru_gates(1)
            for m in range(4):
                tile8("convo1", 0, m, OPA, opa, FILL_A["u2"], False)
            for m in range(KD):
                tile_packed("lruo", m, KR, OPB, opb, FILL_B["yb"])
            for m in range(KD):
                tile8("mix", 0, m, OPA, opa, FILL_A["mix"], m == 0)
                if m:
                    sum_square(NORM["n2"], m - 1)
            sum_square(NORM["n2"], KD - 1)
            broadcast(4)
            ffn(1, NORM["nf"], UPTO != "first", FILL_A["hf1"])
            broadcast(5)
            if UPTO == "first":
                return
            for k in range(KD):
                sum_square(NORM["pre1"], k)
            broadcast(6)
            ffn(2, NORM["post1"], False, FILL_A["hf2"])
            broadcast(7)
            if UPTO == "ffn2":
                return
            for k in range(KD):
                sum_square(NORM["pre2"], k)
            broadcast(8)

            def rows(name, i, ops, fill):
                for j in range(4):
                    bank_free(name, i, j)
                hi, lo = ops
                for k in range(KD):
                    p = PLAN[name][0] + k
                    pe.wait_ge(lo_done, i * 8 + (p + 1 + RING))
                    for j in range(4):
                        c = slice(j * P, (j + 1) * P)
                        out_ps = bank_of(name, j)[:, :]
                        w_hi, w_lo = whi[:, p % SRING, :], wlo[:, p % SRING, :]
                        pe.matmul(out_ps, hi[:, k, c], w_hi, start=k == 0, stop=False)
                        pe.matmul(out_ps, hi[:, k, c], w_lo, start=False, stop=False)
                        mm = pe.matmul(out_ps, lo[:, k, c], w_hi, start=False, stop=k == KD - 1)
                    mm.then_inc(used, 1)

            fill = FILL_A["hmix2"]
            stage8("qka", OPA, opa, fill, 2)
            for i in range(2):
                rows("va", i, OPA, fill)
            for h in range(2):
                panel("low", 0, h, range(4 * h, 4 * h + 4), AUX[:, :], OPA, h == 0, h == 1)
            pe.wait_ge(low_out, 1)
            pe.wait_ge(ld_w2, 16)
            for h in range(GLA_HEADS):
                if h >= 2:
                    pe.wait_ge(la_z, h - 1)
                pe.matmul(bank[6 + h % 2][:, :], wa2[:, h * P:(h + 1) * P], LOW[0:16, :], start=True, stop=True)\
                  .then_inc(la_psum, 1)
            pe.wait_ge(la_z, GLA_HEADS)

            def row_panel(name, i, k, ops):
                hi, lo = ops
                p = PLAN[name][0] + k
                pe.wait_ge(lo_done, i * 8 + (p + 1 + RING))
                for j in range(4):
                    if k == 0:
                        bank_free(name, i, j)
                    c = slice(j * P, (j + 1) * P)
                    out_ps = bank_of(name, j)[:, :]
                    w_hi, w_lo = whi[:, p % SRING, :], wlo[:, p % SRING, :]
                    pe.matmul(out_ps, hi[:, k, c], w_hi, start=k == 0, stop=False)
                    pe.matmul(out_ps, hi[:, k, c], w_lo, start=False, stop=False)
                    mm = pe.matmul(out_ps, lo[:, k, c], w_hi, start=False, stop=k == KD - 1)
                mm.then_inc(used, 1)

            with pe.Fori(0, GLA_HEADS) as i:
                def wait_in(what):
                    pe.wait_ge(gla_in, i * len(GLA_IN) + (GLA_IN.index(what) + 2))

                def wait_cp(what):
                    pe.wait_ge(gla_cp, i * len(GLA_CP) + (GLA_CP.index(what) + 2))

                def wait_exp(what):
                    pe.wait_ge(gla_exp, i * len(GLA_EXP) + (GLA_EXP.index(what) + 2))

                q_h = QK[:, ds(i * 2, 1), :].rearrange("p a t -> p (a t)")
                wait_in("kc")
                for c in range(4):
                    cc = slice(c * P, (c + 1) * P)
                    mm = pe.matmul(bank[6][:, cc], KC[:, cc], q_h[:, cc], start=True, stop=True)
                mm.then_inc(gla_mm, 1)
                row_panel("rv", i, 0, OPA)
                for l in range(1, 8):
                    wait_in(f"q{l}")
                    if l >= 2:
                        wait_cp(f"c{l - 2}")
                    for c in range(4):
                        cc = slice(c * P, (c + 1) * P)
                        mm = pe.matmul(bank[6 + l % 2][:, cc], KQ[:, cc], KQ[:, cc], start=True, stop=True)
                    mm.then_inc(gla_mm, 1)
                    row_panel("rv", i, l, OPA)
                wait_cp("c6")
                wait_in("kd")
                pe.matmul(bank[6][:, 0:3 * P], KQ[:, 0:P], QX[:, 0:3 * P], start=True, stop=True).then_inc(gla_mm, 1)
                wait_cp("c7")
                pe.matmul(bank[7][:, 0:2 * P], KQ[:, P:2 * P], QX[:, 3 * P:5 * P], start=True, stop=True)
                pe.matmul(bank[7][:, 2 * P:3 * P], KQ[:, 2 * P:3 * P], QX[:, 5 * P:6 * P], start=True, stop=True)\
                  .then_inc(gla_mm, 1)
                wait_cp("ao")
                wait_exp("ao")
                place = {(0, 1): 0, (0, 2): 1, (0, 3): 2, (1, 2): 3, (1, 3): 4, (2, 3): 5}
                for t in range(4):
                    out_ps = bank[4 + t // 2][:, t % 2 * GLA_V:(t % 2 + 1) * GLA_V]
                    for j in range(t + 1):
                        a = AD[:, t * P:(t + 1) * P] if j == t else AO[:, place[j, t] * P:(place[j, t] + 1) * P]
                        mm = pe.matmul(out_ps, a, VA[:, j, ds(i * GLA_V, GLA_V)], start=j == 0, stop=j == t)
                    if t % 2:
                        mm.then_inc(gla_mm, 1)

            pe.wait_ge(r_prod, 2 * GLA_HEADS)
            for m in range(KD):
                if m >= 2:
                    pe.wait_ge(b_val, m - 1)
                for t in range(4):
                    mm = pe.transpose(bank[6 + m % 2][:, t * P:(t + 1) * P],
                                      ONH[:, m // 2, t, m % 2 * P:(m % 2 + 1) * P], ident)
                mm.then_inc(oa_t, 1)
            pe.wait_ge(ld_v, 32)
            with pe.Fori(0, FOX_HEADS // 4) as i:
                def scores(u):
                    h, t = u // 4, u % 4
                    n = (t + 1) * P
                    r = slice(FOX_HD * (h % 2), FOX_HD * (h % 2 + 1))
                    s_ps = bank[6 + u % 2][:, 0:n]
                    pe.wait_ge(fox_p, i * 16 + (u + 1))
                    if t == 0:
                        pe.wait_ge(fox_nf, i * 4 + (h + 1))
                    pe.matmul(s_ps, QF[r, 2 * (h // 2), t * P:(t + 1) * P], QF[r, 2 * (h // 2) + 1, 0:n],
                              start=True, stop=False)
                    pe.matmul(s_ps, ones[32:48, :], NFH[32:48, h % 2, 0:n], start=False, stop=True)\
                      .then_inc(fox_s, 1)

                for j in range(4):
                    tile8("qkb", i, j, OPA, opa, fill, False)
                for j in range(4):
                    wait_evac(pe, "qkb", i, j)
                scores(0)
                scores(1)
                for u in range(16):
                    h, t = u // 4, u % 4
                    pe.wait_ge(fox_p, i * 16 + (u + 3))
                    pe.wait_ge(fox_out, i * 16 + (u + 1))
                    for j in range(t + 1):
                        c = slice(j * P, (j + 1) * P)
                        mm = pe.transpose(bank[4 + u % 2][:, c], PR[:, u % 2, c], ident)
                    mm.then_inc(fox_t, 1)
                    if u < 14:
                        scores(u + 2)
                    if u % 4 == 0:
                        bank_free("gab", i, u // 4)
                    k = 2 * (u % 4)
                    panel("gab", i, u // 2, (k, k + 1), bank_of("gab", u // 4)[:, :], OPA, u % 4 == 0, u % 4 == 3,
                          q0=k % 4, done=u % 2 == 1)
                    pe.wait_ge(fox_pt, i * 16 + (u + 3))
                    for j in range(t + 1):
                        mm = pe.matmul(bank[4 + u % 2][:, 0:FOX_HD], PT[:, u % 2, j * P:(j + 1) * P],
                                       VB[:, j, ds(i * (4 * FOX_HD) + h * FOX_HD, FOX_HD)],
                                       start=j == 0, stop=j == t)
                    mm.then_inc(fox_o, 1)
            pe.wait_ge(fox_out, 64 + 2)
            for m in range(KD):
                if m >= 2:
                    pe.wait_ge(opa, FILL_A["ob"] + m - 1)
                else:
                    pe.wait_ge(opb, FILL_B["oa"] + KD)
                for t in range(4):
                    mm = pe.transpose(bank[6 + m % 2][:, t * P:(t + 1) * P], OB[:, t, m * P:(m + 1) * P], ident)
                mm.then_inc(ob_t, 1)
            stage8("pa", OPB, opb, FILL_B["oa"], 2)
            stage8("pb", OPA, opa, FILL_A["ob"], 2)
            for m in range(KD):
                tile8("wout", 0, m, OPB, opb, FILL_B["merged"], m == 0)
                if m:
                    sum_square(NORM["post2"], m - 1)
            sum_square(NORM["post2"], KD - 1)
            broadcast(9)
            for k in range(KD):
                sum_square(NORM["pre3"], k)
            broadcast(10)
            ffn(3, NORM["post3"], False, FILL_A["hf3"])
            broadcast(11)

        @block.vector
        def _(dve):
            own = Steps(dve, vchain)
            stat = [0]
            filled = {"a": 0, "b": 0}

            def settle():
                for s, n in ((opa, filled["a"]), (opb, filled["b"])):
                    if n:
                        dve.wait_ge(s, n)

            def rsqrt(value, n, scale):
                v, y, a, b = (small[:, r, 0:n] for r in range(4))
                own.next(dve.tensor_scalar(v, value, scale, EPS, ALU.mult, ALU.add))
                own.next(dve.tensor_scalar(y.bitcast(I32), v.bitcast(I32), -0.5, float(0x5F3759DF), ALU.mult, ALU.add))
                for _ in range(4):
                    own.next(dve.tensor_tensor(a, y, y, ALU.mult))
                    own.next(dve.scalar_tensor_tensor(out=b, in0=a, scalar=-0.5, in1=v, op0=ALU.mult, op1=ALU.mult))
                    own.next(dve.scalar_tensor_tensor(out=y, in0=b, scalar=1.5, in1=y, op0=ALU.add, op1=ALU.mult))

            RSQRT_STEPS = 14

            def diagonal(y):
                settle()
                for j in range(4):
                    ins = dve.tensor_scalar(tmp[:, 0, j * P:(j + 1) * P], ident, y[:, j:j + 1], None, ALU.mult)
                    if j < 3:
                        own.next(ins)
                ins.then_inc(st_ready, 1)
                stat[0] += 1

            def norm_stat(norm):
                dve.wait_ge(sq_summed, 8 * (norm + 1))
                rsqrt(AUX[:, 0:4], 4, 1.0 / D)
                diagonal(small[:, 1, :])
                dve.wait_ge(bc_ready, stat[0])

            def lo_a(fill, k, shift=None):
                dve.wait_ge(a_hi_w, FILL_A[fill] + k + 1)
                if shift is None:
                    ins = dve.tensor_tensor(a_lo[:, k, :], tmp[:, k % 2, :], a_hi[:, k, :].bitcast(F32), ALU.subtract)
                else:
                    ins = dve.scalar_tensor_tensor(out=a_lo[:, k, :], in0=tmp[:, k % 2, :], scalar=shift(k),
                                                   in1=a_hi[:, k, :].bitcast(F32), op0=ALU.add, op1=ALU.subtract)
                ins.then_inc(opa, 1)

            def operand_a(fill, scale, shift=None):
                for k in range(KD + 1):
                    if k < KD:
                        if k > 1:
                            dve.wait_ge(opa, FILL_A[fill] + k - 1)
                        dve.scalar_tensor_tensor(out=tmp[:, k % 2, :], in0=X[:, k, :], scalar=scale(k), in1=BCAST[:, :],
                                                 op0=ALU.mult, op1=ALU.mult).then_inc(a_val, 1)
                    if k:
                        lo_a(fill, k - 1, shift)
                filled["a"] = FILL_A[fill] + KD

            def ada_block(i, mod0, s):
                dve.wait_ge(ada_landed[s % 2], i * 64 + (64 * mod0 + 16 * (s // 2 + 1)))
                c = small[:, 7, s:s + 1]
                if s == 0:
                    ins = dve.tensor_scalar(ADA_ACC, ADA[:, 0, :], c, None, ALU.mult)
                else:
                    ins = dve.scalar_tensor_tensor(out=ADA_ACC, in0=ADA[:, s % 2, :], scalar=c, in1=ADA_ACC,
                                                   op0=ALU.mult, op1=ALU.add)
                ins.then_inc(ada_used, 1)
                dve.wait_ge(ada_used, i * 8 + (8 * mod0 + s + 3))

            def gate_pair(name, i, pr, at):
                wait_evac(dve, name, i, 2 * pr)
                wait_used(dve, name, i, 4 * pr + 3)
                dve.wait_ge(opb, i * 2 + (at + pr - 1))
                dve.tensor_tensor(tmp[:, pr, :], SIL[:, pr, :], bank_of(name, 2 * pr + 1)[:, :], ALU.mult)\
                   .then_inc(evac_of(name, 2 * pr + 1), 1)
                dve.wait_ge(b_hi_w, i * 2 + (at + pr + 1))
                dve.tensor_tensor(b_lo[:, ds(i * 2 + pr, 1), :].rearrange("p a t -> p (a t)"), tmp[:, pr, :],
                                  b_hi[:, ds(i * 2 + pr, 1), :].rearrange("p a t -> p (a t)").bitcast(F32),
                                  ALU.subtract).then_inc(opb, 1)

            def ffn(n, with_ada):
                for half, K in (("a", FA), ("b", FB)):
                    name = f"gu{n}{half}"
                    turns = K // 2
                    ada_turns = 0 if not with_ada else (6 if half == "a" else 3)
                    at = FILL_B[f"ffn{n}{half}"]
                    mod0 = 0 if half == "a" else 6
                    if ada_turns:
                        with dve.Fori(0, ada_turns) as i:
                            for pr in range(2):
                                for s in range(4 * pr, 4 * pr + 4):
                                    ada_block(i, mod0, s)
                                gate_pair(name, i, pr, at)
                            dve.wait_ge(ada_psum, i + (mod0 + 1))
                            own.begin(i, 1)
                            own.next(dve.tensor_tensor(mods[:, ds(i * 8 + 8 * mod0, 8)], AUX[:, 8:16],
                                                       cols[:, ds(i * 8 + (COLS["b_ada_2"][0] + 8 * mod0), 8)], ALU.add))
                            own.end(ada_turns)
                    if turns > ada_turns:
                        with dve.Fori(ada_turns, turns) as i:
                            for pr in range(2):
                                gate_pair(name, i, pr, at)
                    filled["b"] = at + K
                    name = f"dn{n}{half}"
                    for m in range(KD):
                        if n > 1 and half == "a":
                            break
                        acc = X if n == 1 else Y
                        if n > 1:
                            wait_evac(dve, f"dn{n}a", 0, m)
                        wait_used(dve, name, 0, ((m + 1) * K - 1) // 4)
                        dve.tensor_tensor(acc[:, m, :], acc[:, m, :], bank_of(name, m)[:, :], ALU.add)\
                           .then_inc(evac_of(name, m), 1)

            dve.memset(ones[:, :], 1.0).then_inc(vchain, 1)
            own.n += 1
            dve.wait_ge(vchain, 1)
            for s, n in ((lo_done, RING), (used, SRING), (ada_used, 2)):
                dve.memset(small[:, 4, 0:1], 0.0).then_inc(s, n)
                dve.wait_ge(s, n)
            for s in evac:
                dve.memset(small[:, 4, 0:1], 0.0).then_inc(s, 1)
                dve.wait_ge(s, 1)
            dve.memset(small[:, 5, 0:1], 0.0).then_inc(const_ready, 1)
            dve.wait_ge(ld_c, 48)
            own.next(dve.tensor_copy(masks[:, :, :].rearrange("p a b -> p (a b)"), G[:, S0:S0 + 8 * P]))
            dve.wait_ge(ld_x, 16)
            norm_stat(NORM["n1"])
            operand_a("h1", lambda k: col("norm1_g", k))
            own.next(dve.memset(U[:, :, 0:PAD], 0.0))
            own.next(dve.memset(XR[:, :, 0:LPAD], 0.0))

            dve.wait_ge(lam_e, 1)
            w, w2, acc = (lru_t[:, r, :] for r in (0, 2, 3))
            e = lru_t[:, 1, :]
            own.next(dve.tensor_scalar(w2, e, 2.0, None, ALU.add))
            own.next(dve.reciprocal(acc, w2))
            own.next(dve.tensor_tensor(w, e, acc, ALU.mult))
            own.next(dve.tensor_tensor(w2, w, w, ALU.mult))
            own.next(dve.tensor_scalar(acc, w2, 1.0 / 17, 1.0 / 15, ALU.mult, ALU.add))
            for n in (13, 11, 9, 7, 5, 3, 1):
                own.next(dve.tensor_tensor(acc, acc, w2, ALU.mult))
                own.next(dve.tensor_scalar(acc, acc, 1.0 / n, None, ALU.add))
            own.next(dve.scalar_tensor_tensor(out=acc, in0=acc, scalar=2.0, in1=w, op0=ALU.mult, op1=ALU.mult))
            lam = cols[:, COLS["lru_lambda"][0]:COLS["lru_lambda"][0] + KR]
            own.next(dve.tensor_scalar(w, lam, -1.0, 0.0, ALU.mult, ALU.max))
            own.next(dve.tensor_tensor(w, w, acc, ALU.add))
            own.next(dve.tensor_scalar(lru_c[:, 0, :], w, -8.0, None, ALU.mult))
            own.next(dve.tensor_scalar(lru_c[:, 1, :], w, 8.0, None, ALU.mult))

            def conv_taps(m, lo, hi):
                dst = U[:, ds(m, 1), PAD:U_ST].rearrange("p a t -> p (a t)")
                for k in range(lo, hi):
                    src = U[:, ds(m + 1, 1), k:k + T].rearrange("p a t -> p (a t)")
                    wk = cols[:, ds(m + (COLS["conv_dw_w"][0] + 8 * k), 1)]
                    if k == 0:
                        ins = dve.tensor_scalar(dst, src, wk, cols[:, ds(m + COLS["conv_dw_b"][0], 1)],
                                                ALU.mult, ALU.add)
                    else:
                        ins = dve.scalar_tensor_tensor(out=dst, in0=src, scalar=wk, in1=dst, op0=ALU.mult, op1=ALU.add)
                    if k == TAPS - 1:
                        ins.then_inc(conv_done, 1)
                        dve.wait_ge(conv_done, m + 1)
                    else:
                        own.next(ins)

            with dve.Fori(0, 4) as i:
                own.begin(i, TAPS - 1)
                for pr in range(2):
                    wait_evac(dve, "win", i, 2 * pr + 1)
                    dve.scalar_tensor_tensor(
                        out=U[:, ds(i * 2 + (pr + 1), 1), PAD:U_ST].rearrange("p a t -> p (a t)"), in0=bank[2 * pr][:, :],
                        scalar=cols[:, ds(i * 4 + (COLS["b_in"][0] + 2 * pr), 1)], in1=R5[:, pr, :],
                        op0=ALU.add, op1=ALU.mult).then_inc(evac[2 * pr], 1)
                    wait_evac(dve, "win", i, 2 * pr)
                    conv_taps(i, 0 if pr == 0 else 15, 15 if pr == 0 else TAPS)
                own.end(4)
            with dve.Fori(4, KD) as i:
                own.begin(i - 4, TAPS - 1)
                conv_taps(i, 0, TAPS)
                own.end(KD - 4)
            for m in range(KR):
                wait_evac(dve, "win", 0, 16 + m)
                dst = XR[:, m, LPAD:X_ST]
                for k in range(LTAPS):
                    src = XR[:, m + 1, k:k + T]
                    if k == 0:
                        ins = dve.tensor_scalar(dst, src, col("lru_conv_w", m), col("lru_conv_b", m), ALU.mult, ALU.add)
                    else:
                        ins = dve.scalar_tensor_tensor(out=dst, in0=src, scalar=col("lru_conv_w", KR * k + m), in1=dst,
                                                       op0=ALU.mult, op1=ALU.add)
                    own.next(ins)
                dve.tensor_copy(b_hi[:, m, :], dst).then_inc(b_hi_w, 1)
                dve.wait_ge(b_hi_w, m + 1)
                dve.tensor_tensor(b_lo[:, m, :], dst, b_hi[:, m, :].bitcast(F32), ALU.subtract).then_inc(opb, 1)
            filled["b"] = FILL_B["yb"]
            dve.wait_ge(mean_summed, KD)
            own.next(dve.tensor_scalar(small[:, 1, 0:4], AUX[:, 0:4], 1.0 / D, None, ALU.mult))
            diagonal(small[:, 1, :])
            dve.wait_ge(bc_ready, stat[0])
            for k in range(KD):
                dve.tensor_tensor(U[:, k, PAD:U_ST], U[:, k, PAD:U_ST], BCAST[:, :], ALU.subtract).then_inc(centred, 1)

            def lru_input(half):
                for m in range(5):
                    n = 5 * half + m
                    wait_evac(dve, f"gates{half}", 0, 2 * m + 1)
                    dve.tensor_tensor(XR[:, n, LPAD:X_ST], XR[:, n, LPAD:X_ST], IG[:, n % 2, :], ALU.mult)\
                       .then_inc(ix_done, 1)

            def lru_variance(half):
                for m in range(5):
                    dve.wait_ge(decay, 5 * half + m + 1)
                    if 5 * half + m:
                        dve.wait_ge(var_ready, 5 * half + m)
                    own.next(dve.tensor_tensor(tmp[:, 0, :], A5[m], A5[m], ALU.mult))
                    dve.scalar_tensor_tensor(out=R5[:, m, :], in0=tmp[:, 0, :], scalar=1.0, in1=R5[:, m, :],
                                             op0=ALU.add, op1=ALU.mult).then_inc(var_ready, 1)

            def lru_scan(half):
                for m in range(5):
                    n = 5 * half + m
                    xr = XR[:, n, LPAD:X_ST]
                    dve.wait_ge(root, n + 1)
                    dve.wait_ge(ix_done, n + 1)
                    own.next(dve.tensor_tensor(xr, xr, R5[:, m, :], ALU.mult))
                    own.next(dve.tensor_tensor_scan(tmp[:, 1, :], A5[m], xr, 0.0, ALU.mult, ALU.add))
                    dve.tensor_tensor(RG[:, n, :], tmp[:, 1, :], RG[:, n, :], ALU.mult).then_inc(lru_done, 1)
                    dve.wait_ge(lru_done, n + 1)
                    dve.tensor_copy(b_hi[:, n, :], RG[:, n, :]).then_inc(b_hi_w, 1)
                    dve.wait_ge(b_hi_w, KR + n + 1)
                    dve.tensor_tensor(b_lo[:, n, :], RG[:, n, :], b_hi[:, n, :].bitcast(F32), ALU.subtract)\
                       .then_inc(opb, 1)

            def conv_out(half, m):
                if half == 0 and m == 0:
                    dve.wait_ge(ld_ga, 16)
                wait_used(dve, f"convo{half}", 0, 2 * m + 1)
                g = GA[:, 4 * half + m, :]
                dve.scalar_tensor_tensor(out=g, in0=bank_of(f"convo{half}", m)[:, :], scalar=col("conv_b_out", 4 * half + m),
                                         in1=g, op0=ALU.add, op1=ALU.mult).then_inc(evac_of(f"convo{half}", m), 1)

            lru_input(0)
            norm_stat(NORM["ln"])
            for k in range(KD + 1):
                if k < KD:
                    if k > 1:
                        dve.wait_ge(opa, FILL_A["u2"] + k - 1)
                    dve.scalar_tensor_tensor(out=tmp[:, k % 2, :], in0=U[:, k, PAD:U_ST], scalar=col("conv_ln_g", k),
                                             in1=BCAST[:, :], op0=ALU.mult, op1=ALU.mult).then_inc(a_val, 1)
                if k:
                    dve.wait_ge(u_silu, k)
                    dve.tensor_copy(a_hi[:, k - 1, :], tmp[:, (k - 1) % 2, :]).then_inc(a_hi_w, 1)
                    lo_a("u2", k - 1)
            filled["a"] = FILL_A["u2"] + KD
            settle()
            lru_variance(0)
            for m in range(4):
                conv_out(0, m)
            lru_scan(0)
            lru_input(1)
            lru_variance(1)
            conv_out(1, 0)
            conv_out(1, 1)
            lru_scan(1)
            conv_out(1, 2)
            conv_out(1, 3)
            dve.wait_ge(ld_gb, 16)
            for m in range(KD + 1):
                if m < KD:
                    if m > 1:
                        dve.wait_ge(opa, FILL_A["mix"] + m - 1)
                    wait_used(dve, "lruo", 0, ((m + 1) * KR - 1) // 4)
                    dve.tensor_tensor(tmp[:, m % 2, :], bank_of("lruo", m)[:, :], GB[:, m, :], ALU.mult)\
                       .then_inc(evac_of("lruo", m), 1)
                    wait_evac(dve, "lruo", 0, m)
                    if m == 0:
                        wait_evac(dve, "convo1", 0, 3)
                    dve.tensor_tensor(tmp[:, m % 2, :], tmp[:, m % 2, :], GA[:, m, :], ALU.add).then_inc(a_val, 1)
                if m:
                    lo_a("mix", m - 1)
            filled["a"], filled["b"] = FILL_A["mix"] + KD, FILL_B["yb"] + KR
            dve.wait_ge(ld_x2, 16)
            for m in range(KD):
                wait_used(dve, "mix", 0, 2 * m + 1)
                dve.tensor_tensor(X[:, m, :], X[:, m, :], bank_of("mix", m)[:, :], ALU.add)\
                   .then_inc(evac_of("mix", m), 1)
            norm_stat(NORM["n2"])
            operand_a("hf1", lambda k: col("norm2_g", k))
            ffn(1, UPTO != "first")
            norm_stat(NORM["nf"])
            for k in range(KD):
                dve.scalar_tensor_tensor(out=X[:, k, :], in0=X[:, k, :], scalar=col("norm_f_g", k), in1=BCAST[:, :],
                                         op0=ALU.mult, op1=ALU.mult).then_inc(x_ready, 1)
            if UPTO == "first":
                return

            for b in range(3):
                own.next(dve.scalar_tensor_tensor(
                    out=derived[:, b, :], in0=mods[:, 24 * b + 8:24 * b + 16], scalar=1.0,
                    in1=cols[:, COLS["g_pre_2"][0] + 8 * b:COLS["g_pre_2"][0] + 8 * b + 8], op0=ALU.add, op1=ALU.mult))
                own.next(dve.scalar_tensor_tensor(
                    out=derived[:, 3 + b, :], in0=mods[:, 24 * b + 16:24 * b + 24], scalar=1.0 if b == 1 else 0.5,
                    in1=cols[:, COLS["g_post_2"][0] + 8 * b:COLS["g_post_2"][0] + 8 * b + 8], op0=ALU.mult, op1=ALU.mult))

            def residual(b):
                for k in range(KD):
                    own.next(dve.scalar_tensor_tensor(out=Y[:, k, :], in0=Y[:, k, :], scalar=derived[:, 3 + b, k:k + 1],
                                                      in1=BCAST[:, :], op0=ALU.mult, op1=ALU.mult))
                    dve.tensor_tensor(X[:, k, :], X[:, k, :], Y[:, k, :], ALU.add).then_inc(x_ready, 1)

            def modulated(b, fill):
                operand_a(fill, lambda k: derived[:, b, k:k + 1], lambda k: mods[:, 24 * b + k:24 * b + k + 1])

            norm_stat(NORM["pre1"])
            modulated(0, "hf2")
            ffn(2, False)
            norm_stat(NORM["post1"])
            residual(0)
            if UPTO == "ffn2":
                return
            norm_stat(NORM["pre2"])
            modulated(1, "hmix2")

            own.next(dve.memset(RESET, 1.0))
            own.next(dve.memset(RESET.rearrange("p (n m) -> p n m", m=P)[:, :, 0:1], 0.0))
            for s, n in ((gla_in, 1), (gla_cp, 1), (fox_out, 2), (fox_t, 2), (fox_o, 2), (fox_pt, 2), (fox_p, 2)):
                dve.memset(small[:, 4, 0:1], 0.0).then_inc(s, n)
                dve.wait_ge(s, n)
            for s, n in ((gla_exp, 1), (gla_mm, 1), (rows_out[0], 16), (rows_out[1], 16)):
                dve.memset(small[:, 4, 0:1], 0.0).then_inc(s, n)
                dve.wait_ge(s, n)
            for h in range(GLA_HEADS):
                dve.wait_ge(la_ln, h + 1)
                own.next(dve.scalar_tensor_tensor(out=LA[:, h, :], in0=LA[:, h, :], scalar=0.0, in1=LT[:, h, :],
                                                  op0=ALU.min, op1=ALU.subtract))
            f_log, f_sum = LOW[32:48, :], LT[32:48, 4, :]
            dve.wait_ge(la_ln, 5)
            own.next(dve.scalar_tensor_tensor(out=f_log, in0=f_log, scalar=0.0, in1=f_sum, op0=ALU.min,
                                              op1=ALU.subtract))
            own.next(dve.tensor_tensor_scan(f_sum, ones[32:48, 0:1].to_broadcast([16, T]), f_log, 0.0, ALU.mult, ALU.add))
            own.next(dve.tensor_scalar(f_log, f_sum, -1.0, None, ALU.mult))

            with dve.Fori(0, GLA_HEADS) as i:
                made, copied = [0], [0]

                def give(label, ins):
                    assert GLA_IN[made[0]] == label, (GLA_IN[made[0]], label)
                    made[0] += 1
                    ins.then_inc(gla_in, 1)
                    dve.wait_ge(gla_in, i * len(GLA_IN) + (made[0] + 1))

                def copy(label, ins):
                    assert GLA_CP[copied[0]] == label, (GLA_CP[copied[0]], label)
                    copied[0] += 1
                    ins.then_inc(gla_cp, 1)
                    dve.wait_ge(gla_cp, i * len(GLA_CP) + (copied[0] + 1))

                def wait_exp(what):
                    dve.wait_ge(gla_exp, i * len(GLA_EXP) + (GLA_EXP.index(what) + 2))

                def wait_mm(what):
                    dve.wait_ge(gla_mm, i * len(GLA_MM) + (GLA_MM.index(what) + 2))

                q_h = QK[:, ds(i * 2, 1), :].rearrange("p a t -> p (a t)")
                k_h = QK[:, ds(i * 2 + 1, 1), :].rearrange("p a t -> p (a t)")

                def blocks(x, l):
                    return x.rearrange("p (n m) -> p n m", m=2 * (P >> l))

                def below(l):
                    m = P >> l
                    b = blocks(BC, l)
                    return dve.tensor_tensor(blocks(E2[l % 2], l), b, b[:, :, m - 1:m].to_broadcast([P, T // (2 * m), 2 * m]),
                                             ALU.subtract)

                def level(l):
                    wait_mm(f"m{l}")
                    dve.memset(small[:, 4, 1:2], 0.0)
                    copy(f"c{l}", dve.copy_predicated(
                        AD.rearrange("p (c t) -> p c t", t=P),
                        masks[:, l:l + 1, :].to_broadcast([P, 4, P]),
                        bank[6 + l % 2][:, :].rearrange("p (c t) -> p c t", t=P)))

                give("bc", dve.tensor_tensor_scan(BC, RESET, LA[:, ds(i, 1), :].rearrange("p a t -> p (a t)"), 0.0,
                                                  ALU.mult, ALU.add))
                give("kc", dve.tensor_copy(KC, k_h))
                copy("ms", dve.memset(AD, 0.0))
                give("d1", below(1))
                level(0)
                give("d2", below(2))
                for l in range(1, 8):
                    m = P >> l
                    wait_exp(f"ef{l}")
                    give(f"k{l}", dve.tensor_tensor(blocks(KQ, l)[:, :, 0:m], blocks(k_h, l)[:, :, 0:m],
                                                    blocks(E2[l % 2], l)[:, :, 0:m], ALU.mult))
                    wait_exp(f"es{l}")
                    give(f"q{l}", dve.tensor_tensor(blocks(KQ, l)[:, :, m:], blocks(q_h, l)[:, :, m:],
                                                    blocks(E2[l % 2], l)[:, :, m:], ALU.mult))
                    if l < 6:
                        give(f"d{l + 2}", below(l + 2))
                    elif l == 6:
                        b = BC.rearrange("p (n m) -> p n m", m=P)
                        give("do", dve.tensor_tensor(E2[0].rearrange("p (n m) -> p n m", m=P),
                                                     b[:, :, P - 1:P].to_broadcast([P, 4, P]), b, ALU.subtract))
                    level(l)
                for n, (at, c) in enumerate(((0, 1), (3, 2), (5, 3))):
                    give(f"x{n}", dve.tensor_tensor(QX[:, at * P:(at + 1) * P], q_h[:, c * P:(c + 1) * P],
                                                    EB[:, c * P:(c + 1) * P], ALU.mult))
                for n, (at, src, c) in enumerate(((4, 5, 2), (1, 3, 1), (2, 4, 1))):
                    give(f"x{n + 3}", dve.tensor_scalar(QX[:, at * P:(at + 1) * P], QX[:, src * P:(src + 1) * P],
                                                        EB[:, (c + 1) * P - 1:(c + 1) * P], None, ALU.mult))
                wait_exp("eo")
                give("kd", dve.tensor_tensor(KQ[:, 0:3 * P], k_h[:, 0:3 * P], E2[0][:, 0:3 * P], ALU.mult))
                wait_mm("o0")
                copy("ao", dve.tensor_copy(AO[:, 0:3 * P], bank[6][:, 0:3 * P]))
                wait_exp("sq3")
                own.begin(i, RSQRT_STEPS)
                rsqrt(small[:, 5, 0:4], 4, 1.0 / GLA_V)
                own.end(GLA_HEADS)
                give("y", dve.tensor_copy(small[:, 6, 0:4], small[:, 1, 0:4]))
                assert made[0] == len(GLA_IN) and copied[0] == len(GLA_CP)

            for t in range(4):
                dve.wait_ge(r_silu, t + 1)
                dve.wait_ge(gla_exp, GLA_HEADS * len(GLA_EXP) + 1)
                for g in range(2):
                    v = ONH[:, 2 * g:2 * g + 2, t, :]
                    dve.tensor_tensor(v, v, R2[:, t, g * SOME:(g + 1) * SOME].rearrange("p (h e) -> p h e", h=2), ALU.mult)\
                       .then_inc(r_prod, 1)
            for j in range(2):
                dve.wait_ge(rows_out[j], 16 * (2 * GLA_HEADS + 1))
            for m in range(KD):
                dve.wait_ge(oa_t, m + 1)
                if m >= 2:
                    dve.wait_ge(opb, FILL_B["oa"] + m - 1)
                dve.tensor_scalar(tmp[:, m % 2, :], bank[6 + m % 2][:, :], col("g_gla_2", m), None, ALU.mult)\
                   .then_inc(b_val, 1)
                dve.wait_ge(b_hi_w, FILL_B["oa"] + m + 1)
                dve.tensor_tensor(b_lo[:, m, :], tmp[:, m % 2, :], b_hi[:, m, :].bitcast(F32), ALU.subtract)\
                   .then_inc(opb, 1)

            with dve.Fori(0, FOX_HEADS // 4) as i:
                def maximum(u):
                    h, t = u // 4, u % 4
                    if t == 0:
                        if h >= 2:
                            dve.wait_ge(fox_s, i * 16 + (u - 4))
                        dve.tensor_scalar(NFH[32:48, h % 2, :], LOW[32:48, :],
                                          consts[32:48, 0, ds(i * 4 + (32 + h), 1)], None, ALU.mult)\
                           .then_inc(fox_nf, 1)
                    s_ps = bank[6 + u % 2]
                    dve.wait_ge(fox_s, i * 16 + (u + 1))
                    own.next(dve.tensor_tensor(s_ps[:, t * P:(t + 1) * P], s_ps[:, t * P:(t + 1) * P], tri, ALU.add))
                    own.next(dve.tensor_reduce(small[:, 0, u % 2:u % 2 + 1], s_ps[:, 0:(t + 1) * P], AX_X, ALU.max))
                    dve.tensor_scalar(small[:, 6, t:t + 1], small[:, 0, u % 2:u % 2 + 1], -1.0, None, ALU.mult)\
                       .then_inc(fox_m, 1)

                own.begin(i, 16 * 3)
                maximum(0)
                maximum(1)
                for u in range(16):
                    h, t = u // 4, u % 4
                    if u < 14:
                        maximum(u + 2)
                    dve.wait_ge(fox_o, i * 16 + (u + 3))
                    own.next(dve.reciprocal(small[:, 1, u % 2:u % 2 + 1], small[:, 5, t:t + 1]))
                    dve.tensor_scalar(OB[:, t, ds(i * (4 * FOX_HD) + h * FOX_HD, FOX_HD)],
                                      bank[4 + u % 2][:, 0:FOX_HD], small[:, 1, u % 2:u % 2 + 1], None, ALU.mult)\
                       .then_inc(fox_out, 1)
                own.end(FOX_HEADS // 4)
            for m in range(KD):
                dve.wait_ge(a_hi_w, FILL_A["ob"] + m + 1)
                dve.tensor_tensor(a_lo[:, m, :], bank[6 + m % 2][:, :], a_hi[:, m, :].bitcast(F32), ALU.subtract)\
                   .then_inc(opa, 1)
            for m in range(KD):
                wait_used(dve, "pa", 0, 2 * m + 1)
                dve.wait_ge(gate2, m + 1)
                dve.tensor_tensor(GA2[:, m, :], bank_of("pa", m)[:, :], GA2[:, m, :], ALU.mult)\
                   .then_inc(evac_of("pa", m), 1)
            for m in range(KD + 1):
                if m < KD:
                    wait_used(dve, "pb", 0, 2 * m + 1)
                    dve.wait_ge(gate2, KD + m + 1)
                    dve.wait_ge(opb, FILL_B["merged"] + m - 1)
                    dve.tensor_tensor(tmp[:, m % 2, :], bank_of("pb", m)[:, :], GB2[:, m, :], ALU.mult)\
                       .then_inc(evac_of("pb", m), 1)
                    wait_evac(dve, "pb", 0, m)
                    wait_evac(dve, "pa", 0, m)
                    dve.tensor_tensor(tmp[:, m % 2, :], tmp[:, m % 2, :], GA2[:, m, :], ALU.add).then_inc(b_val, 1)
                if m:
                    dve.wait_ge(b_hi_w, FILL_B["merged"] + m)
                    dve.tensor_tensor(b_lo[:, m - 1, :], tmp[:, (m - 1) % 2, :], b_hi[:, m - 1, :].bitcast(F32),
                                      ALU.subtract).then_inc(opb, 1)
            filled["a"], filled["b"] = FILL_A["ob"] + KD, FILL_B["merged"] + KD
            norm_stat(NORM["post2"])
            residual(1)
            norm_stat(NORM["pre3"])
            modulated(2, "hf3")
            ffn(3, False)
            norm_stat(NORM["post3"])
            residual(2)


def lay_panels(w):
    import numpy as np
    K, N = w.shape
    t = w.reshape(K // P, P, N // P, P).transpose(2, 0, 1, 3).reshape(-1, P, P)
    if t.shape[0] % 4:
        t = np.concatenate([t, np.zeros((4 - t.shape[0] % 4, P, P), t.dtype)])
    return t.reshape(-1, 4, P, P).transpose(0, 2, 1, 3).reshape(-1, P, SOME)


def lay_rows(w):
    K, N = w.shape
    return w.reshape(K // P, P, N // SOME, SOME).transpose(2, 0, 1, 3).reshape(-1, P, SOME)


def alternate(a, b):
    import numpy as np
    K, N = a.shape
    return np.stack([a.reshape(K, N // P, P), b.reshape(K, N // P, P)], 2).reshape(K, 2 * N)


def turns(a, b):
    import numpy as np
    return np.stack([a.reshape(-1, 8, P, SOME), b.reshape(-1, 8, P, SOME)], 1).reshape(-1, P, SOME)


def lay_gates(wa, wx, half):
    import numpy as np
    out = []
    for m in range(5 * half, 5 * half + 5):
        for w in (wa, wx):
            full = np.zeros((D_RNN + 2 * P, P), w.dtype)
            for h in range(HEADS_LRU):
                lo, hi = h * LRU_BLOCK, (h + 1) * LRU_BLOCK
                a, b = max(lo, m * P), min(hi, (m + 1) * P)
                if a < b:
                    full[P + lo:P + hi, a - m * P:b - m * P] = w[h][:, a - lo:b - lo]
            blocks = np.concatenate([full[m * P:(m + 3) * P], np.zeros((P, P), w.dtype)]).reshape(4, P, P)
            out.append(blocks.transpose(1, 0, 2).reshape(P, SOME))
    return np.stack(out)


def kernel(**inputs):
    import numpy as np
    import concourse.bacc as bacc
    from concourse.bass_utils import run_bass_kernel_spmd as run

    v = {n: np.asarray(a) for n, a in inputs.items()}
    w_in = v["w_in"][0]
    cuts = [0, D, 2 * D, 2 * D + D_RNN, 2 * D + 2 * D_RNN]
    parts = [lay_panels(alternate(w_in[:, 0:D], w_in[:, D:2 * D])), lay_panels(w_in[:, 2 * D:]),
             lay_gates(v["lru_wa"][0], v["lru_wx"][0], 0), lay_panels(v["conv_w_out"][0][:, :D // 2]),
             lay_gates(v["lru_wa"][0], v["lru_wx"][0], 1), lay_panels(v["conv_w_out"][0][:, D // 2:]),
             lay_panels(v["lru_w_out"][0]), lay_panels(v["w_mix_out"][0])]

    def ffn_panels(g, u, dn):
        a = FA * P
        return [lay_panels(alternate(g[:, :a], u[:, :a])), lay_panels(dn[:a]),
                lay_panels(alternate(g[:, a:], u[:, a:])), lay_panels(dn[a:])]

    parts += ffn_panels(v["ffn_w1"][0], v["ffn_w3"][0], v["ffn_w2"][0])
    parts += ffn_panels(v["w_gu1_2"][0][:, :FF], v["w_gu1_2"][0][:, FF:], v["w_dn1_2"][0])
    w2 = v["w_in_2"][0]
    at = np.cumsum([0, 512, 512, 1024, 16, 1024, 1024, 1024, 1024, 16, 1024, 1024])
    q_a, k_a, v_a, a_low, r_a, q_b, k_b, v_b, f_b, gate_a, gate_b = (w2[:, at[i]:at[i + 1]] for i in range(11))
    low = np.zeros((D, P), w2.dtype)
    low[:, 0:16] = a_low
    low[:, 32:48] = f_b
    parts += [lay_panels(np.concatenate([q_a, k_a], 1)), lay_rows(v_a), lay_panels(low), lay_rows(r_a),
              lay_rows(v_b), turns(lay_panels(alternate(q_b, k_b)), lay_panels(np.concatenate([gate_a, gate_b], 1))),
              lay_panels(v["w_pa_2"][0]), lay_panels(v["w_pb_2"][0]), lay_panels(v["w_out_2"][0])]
    parts += ffn_panels(v["w_gu2_2"][0][:, :FF], v["w_gu2_2"][0][:, FF:], v["w_dn2_2"][0])
    stream = np.concatenate(parts)[:NPANELS]
    ada = v["w_ada_2"][0].reshape(KD, P, 9, D).transpose(2, 0, 1, 3).reshape(-1, P, D)

    def as_cols(a):
        return a.reshape(-1, P).T

    b_in = v["b_in"][0]
    glu_bias = np.stack([b_in[:D].reshape(-1, P), b_in[D:2 * D].reshape(-1, P)], 1).reshape(-1)
    given = dict(v)
    given["b_in"] = np.concatenate([glu_bias, b_in[2 * D:]])
    columns = []
    for n, (start, count) in COLS.items():
        if n == "b_f_2":
            c = np.zeros((P, 1), np.float32)
            c[32:48, 0] = v[n][0]
        else:
            c = as_cols(given[n])
        assert c.shape == (P, count), (n, c.shape)
        columns.append(c)
    cols = np.concatenate(columns, 1)
    consts = np.stack([np.eye(P, dtype=np.float32), np.triu(np.full((P, P), -1e30, np.float32), 1)], 1)
    s_, t_ = np.arange(P)[:, None], np.arange(P)[None, :]
    masks = [s_ == t_]
    for l in range(1, 8):
        m = P >> l
        masks.append((s_ // (2 * m) == t_ // (2 * m)) & (s_ // m % 2 == 0) & (t_ // m % 2 == 1))
    masks = np.stack(masks, 1).astype(np.float32)

    nc = bacc.Bacc("TRN2", target_bir_lowering=False, num_devices=1)
    arrays = {"stream": stream, "ada": ada, "x": v["x"][0].T.reshape(KD, P, T).transpose(1, 0, 2), "cols": cols,
              "consts": consts, "masks": masks, "wa2": v["w_a2_2"][0]}
    arrays = {n: np.ascontiguousarray(a) for n, a in arrays.items()}
    args = [nc.dram_tensor(f"d_{n}", a.shape, mybir.dt.from_np(a.dtype), kind="ExternalInput").ap() for n, a in arrays.items()]
    args.append(nc.dram_tensor("d_out", (P, KD, T), F32, kind="ExternalOutput").ap())
    args += [nc.dram_tensor(f"spill_{n}", (P, KD, T), F32, kind="Internal").ap() for n in ("ga", "gb")]
    args.append(nc.dram_tensor("spill_rv", (P, 2 * KD, T), F32, kind="Internal").ap())
    build(nc, *args)
    r = run(nc, [{f"d_{n}": a for n, a in arrays.items()}], core_ids=[0])
    y = r.results[0]["d_out"]
    return y.transpose(1, 0, 2).reshape(D, T).T[None]
```

```python
from contextlib import ExitStack

import concourse.bass as bass
from concourse import mybir

F32 = mybir.dt.float32
F32R = mybir.dt.float32r
I32 = mybir.dt.int32
U8 = mybir.dt.uint8
ACT = mybir.ActivationFunctionType
ALU = mybir.AluOpType
AX_X = mybir.AxisListType.X
ds = bass.ds

P = 128
T = 512
D = 1024
KD = D // P
D_RNN = 1280
KR = D_RNN // P
HEADS_LRU, LRU_BLOCK = 16, 80
TAPS, LTAPS = 31, 4
FF = 2816
FA, FB = 12, 10
PAD, LPAD = TAPS - 1, LTAPS - 1
EPS = 1e-6
GLA_HEADS, GLA_V = 4, 256
FOX_HEADS, FOX_HD = 16, 64
TAU = 16.0
RING, SRING, AHEAD = 8, 4, 3
SOME = 4 * P

def k_panels(K, tiles):
    return -(-K * tiles // 4)


def make_plan():
    ffn = lambda n: [(f"gu{n}a", 4 * FA, 2 * FA), (f"dn{n}a", k_panels(FA, KD), KD),
                     (f"gu{n}b", 4 * FB, 2 * FB), (f"dn{n}b", k_panels(FB, KD), KD)]
    order = [("win", 104, 52), ("gates0", 10, 10), ("convo0", 8, 4), ("gates1", 10, 10), ("convo1", 8, 4),
             ("lruo", k_panels(KR, KD), KD), ("mix", 16, 8)] + ffn(1) + ffn(2)
    order += [("qka", 16, 8), ("low", 2, 0), ("va", 16, 8), ("rv", 64, 32), ("qkb", 32, 16),
              ("pa", 16, 8), ("pb", 16, 8), ("wout", 16, 8)] + ffn(3)
    plan, p, t = {}, 0, 0
    for name, panels, tiles in order:
        plan[name] = (p, t, panels, tiles)
        p += panels
        t += tiles
    total = p
    p, t, panels, tiles = plan["rv"]
    plan["gab"] = (p + 8, t + 4, panels, tiles)
    return plan, total


PER_TURN = {"rv": (16, 2), "gab": (16, 2)}


def per_turn(name):
    return PER_TURN.get(name, (8, 1))


PLAN, NPANELS = make_plan()
X_FINAL = 3 * KD

COLS = {}
NCOLS = 0
for _n, _c in [("norm1_g", 8), ("b_in", 52), ("conv_dw_w", TAPS * 8), ("conv_dw_b", 8), ("conv_ln_g", 8),
               ("conv_ln_b", 8), ("conv_b_out", 8), ("lru_conv_w", LTAPS * 10), ("lru_conv_b", 10),
               ("lru_ba", 10), ("lru_bx", 10), ("lru_lambda", 10), ("norm2_g", 8), ("norm_f_g", 8),
               ("c_2", 8), ("b_ada_2", 72), ("g_pre_2", 24), ("g_post_2", 24), ("b_a_2", 4), ("g_gla_2", 8),
               ("b_f_2", 1)]:
    COLS[_n] = (NCOLS, _c)
    NCOLS += _c

FILL_A = {n: 8 * i for i, n in enumerate(["h1", "u2", "mix", "hf1", "hf2", "hmix2", "ob", "hf3"])}
FILL_B = {}
_b = 0
for _n, _c in [("xb", 10), ("yb", 10), ("ffn1a", FA), ("ffn1b", FB), ("ffn2a", FA), ("ffn2b", FB), ("oa", 8),
               ("merged", 8), ("ffn3a", FA), ("ffn3b", FB)]:
    FILL_B[_n] = _b
    _b += _c
NORM = {n: i for i, n in enumerate(["n1", "ln", "n2", "nf", "post1", "pre2", "post2", "pre3", "post3"])}


GLA_IN = ["bc", "kc", "d1", "d2"]
for _l in range(1, 8):
    GLA_IN += [f"k{_l}", f"q{_l}"] + ([f"d{_l + 2}"] if _l < 6 else ["do"] if _l == 6 else [])
GLA_IN += [f"x{_n}" for _n in range(6)] + ["kd", "y"]
GLA_EXP = ["eb"]
for _l in range(1, 8):
    GLA_EXP += [f"ef{_l}", f"es{_l}"]
GLA_EXP += ["eo", "ao"] + [f"sq{_n}" for _n in range(4)] + [f"on{_n}" for _n in range(4)]
GLA_MM = [f"m{_l}" for _l in range(8)] + ["o0", "o1", "pv0", "pv1"]
GLA_CP = ["ms"] + [f"c{_l}" for _l in range(8)] + ["ao"]


def build(nc, stream, ada, xT, cols_d, consts_d, masks_d, wa2_d, out, spill_ga, spill_gb, spill_rv):
    ctx = ExitStack()
    with ctx:
        def sb(name, shape, dt=F32):
            return ctx.enter_context(nc.sbuf_tensor(name, shape, dt))

        def sem(name):
            return ctx.enter_context(nc.semaphore(name))

        raw = sb("raw", [P, RING, SOME])
        whi = sb("whi", [P, SRING, SOME], F32R)
        wlo = sb("wlo", [P, SRING, SOME], F32R)
        a_hi = sb("a_hi", [P, KD, T], F32R)
        a_lo = sb("a_lo", [P, KD, T], F32R)
        b_hi = sb("b_hi", [P, FA, T], F32R)
        b_lo = sb("b_lo", [P, FA, T], F32R)
        U_ST, X_ST = PAD + T, LPAD + T
        XR0 = (KD + 1) * U_ST
        X0 = XR0 + (KR + 1) * X_ST
        S0 = X0 + KR * T
        G_END = S0 + 9 * T
        G = sb("G", [P, G_END])
        sq = sb("sq", [P, 2, T])
        tmp = sb("tmp", [P, 2, T])
        cols = sb("cols", [P, NCOLS])
        consts = sb("consts", [P, 2, P])
        ones = sb("ones", [P, P])
        masks = sb("masks", [P, 8, P], U8)
        small = sb("small", [P, 8, 16])
        mods = sb("mods", [P, 72])
        derived = sb("derived", [P, 7, 8])
        one_g2 = sb("one_g2", [P, KD, 2])
        lru_c = sb("lru_c", [P, 2, 10])
        lru_t = sb("lru_t", [P, 4, 10])
        ident = consts[:, 0, :]
        tri = consts[:, 1, :]

        def col(name, k):
            at, n = COLS[name]
            return cols[:, at + k:at + k + 1] if isinstance(k, int) else cols[:, ds(k + at, 1)]

        def tiles(at, n):
            return G[:, at:at + n * T].rearrange("p (n t) -> p n t", t=T)

        X = tiles(X0, KD)
        U = G[:, 0:XR0].rearrange("p (n t) -> p n t", t=U_ST)
        XR = G[:, XR0:X0].rearrange("p (n t) -> p n t", t=X_ST)
        RG = tiles(X0, KR)
        R5 = tiles(S0, 5)
        IG = tiles(S0 + 5 * T, 2)
        AR = tiles(S0 + 7 * T, 2)
        STG = tiles(S0, 2)
        GA = tiles(0, KD)
        GB = tiles(XR0, KD)
        Y = tiles(0, KD)
        A5 = [AR[:, 0, :], AR[:, 1, :], G[:, KD * T:(KD + 1) * T], sq[:, 0, :], sq[:, 1, :]]
        ADA = G[:, KD * T:KD * T + 2 * D].rearrange("p (n t) -> p n t", t=D)
        ADA_ACC = G[:, KD * T + 2 * D:KD * T + 3 * D]
        SIL = tiles(KD * T + 3 * D, 2)
        QK = tiles(0, 8)
        LA = tiles(8 * T, 4)
        VA = G[:, 12 * T:20 * T].rearrange("p (n t) -> p n t", t=D)
        B0 = X0 + KD * T
        BC, KC, EE, EB, KQ, AD = (G[:, B0 + i * T:B0 + (i + 1) * T] for i in range(6))
        QX = G[:, B0 + 6 * T:B0 + 6 * T + 6 * P]
        AO = G[:, B0 + 6 * T + 6 * P:B0 + 6 * T + 12 * P]
        ON = G[:, B0 + 9 * T:B0 + 11 * T].rearrange("p (n t) -> p n t", t=GLA_V)
        LT = tiles(B0, 5)
        wa2 = G[0:16, B0 + 5 * T:B0 + 6 * T]
        RESET, LOW = sq[:, 0, :], sq[:, 1, :]
        E2 = [KC, EE]
        ONH = G[:, 0:8 * T].rearrange("p (h t e) -> p h t e", h=GLA_HEADS, e=GLA_V)
        R2 = G[:, B0:B0 + 8 * T].rearrange("p (n t) -> p n t", t=D)
        VB = VA
        OB = G[:, 0:8 * T].rearrange("p (n t) -> p n t", t=D)
        QF = tiles(8 * T, 4)
        PR, PT = tiles(B0, 2), tiles(B0 + 2 * T, 2)
        FHL, FLO, NFH, ONES_R = b_lo[:, 9, :], b_lo[32:48, 10, :], b_hi[:, 8:10, :], b_lo[:, 8, 0:P]
        GA2, GB2 = tiles(12 * T, KD), tiles(B0, KD)
        assert B0 + 11 * T <= G_END and 20 * T <= X0

        SQ8, PAIRS = tiles(8 * T, KD), tiles(16 * T, 4)
        SQ_ACC = tmp[:, 1, :]

        bank = [ctx.enter_context(nc.psum_tensor(f"bank{i}", [P, T], F32)) for i in range(8)]
        AUX, BCAST = bank[4], bank[5]

        raw_landed = [sem(f"raw_landed{i}") for i in range(RING)]
        hi_done = sem("hi_done")
        lo_done = sem("lo_done")
        used = sem("used")
        evac = [sem(f"evac{i}") for i in range(4)]
        a_val, a_hi_w, opa = sem("a_val"), sem("a_hi_w"), sem("opa")
        b_val, b_hi_w, opb = sem("b_val"), sem("b_hi_w"), sem("opb")
        ld_x = [sem(f"ld_x_{i}") for i in range(4)]
        ld_c, ld_m, ld_w2, ld_ga, ld_gb, ld_x2 = (sem(f"ld_{n}") for n in ("c", "m", "w2", "ga", "gb", "x2"))
        vchain = sem("vchain")
        achain = sem("achain")
        const_ready = sem("const_ready")
        sq_ready = sem("sq_ready")
        sq_summed = sem("sq_summed")
        pair_ready = sem("pair_ready")
        conv_added = sem("conv_added")
        mean_summed = sem("mean_summed")
        st_ready = sem("st_ready")
        bc_ready = sem("bc_ready")
        x_ready = sem("x_ready")
        stage_out = [sem("stage_out0"), sem("stage_out1")]
        conv_done = sem("conv_done")
        centred = sem("centred")
        u_silu = sem("u_silu")
        ix_done = sem("ix_done")
        decay = sem("decay")
        var_ready = sem("var_ready")
        root = sem("root")
        lru_done = sem("lru_done")
        lam_e, silc = sem("lam_e"), sem("silc")
        ada_landed = [sem("ada_landed0"), sem("ada_landed1")]
        ada_used = sem("ada_used")
        ada_psum = sem("ada_psum")
        out_done = sem("out_done")
        low_out = sem("low_out")
        la_psum, la_z, la_ln = sem("la_psum"), sem("la_z"), sem("la_ln")
        gla_in = sem("gla_in")
        gla_exp = sem("gla_exp")
        gla_mm = sem("gla_mm")
        gla_cp = sem("gla_cp")
        fox_nf, fox_s, fox_m, fox_p, fox_t, fox_pt, fox_o, fox_out = (
            sem(f"fox_{n}") for n in ("nf", "s", "m", "p", "t", "pt", "o", "out"))
        ob_t = sem("ob_t")
        rows_out = [sem("rows_out0"), sem("rows_out1")]
        gate2 = sem("gate2")
        f_split, ld_f = sem("f_split"), sem("ld_f")
        ld_r, r_silu = sem("ld_r"), sem("r_silu")
        r_prod = sem("r_prod")
        oa_t = sem("oa_t")
        ld_v = sem("ld_v")

        class Steps:
            def __init__(self, eng, s):
                self.eng, self.s, self.n, self.i, self.per = eng, s, 0, None, 0

            def next(self, ins):
                self.n += 1
                ins.then_inc(self.s, 1)
                self.eng.wait_ge(self.s, self.n if self.i is None else self.i * self.per + self.n)

            def behind(self, ins):
                self.n += 1
                ins.then_inc(self.s, 1)
                self.eng.wait_ge(self.s, self.n - 1 if self.i is None else self.i * self.per + self.n - 1)

            def all(self):
                self.eng.wait_ge(self.s, self.n if self.i is None else self.i * self.per + self.n)

            def begin(self, i, per):
                self.i, self.per, self.at = i, per, self.n

            def end(self, turns):
                assert self.n - self.at == self.per, (self.n - self.at, self.per)
                self.n += self.per * (turns - 1)
                self.i = None

        def wait_used(eng, name, i, s):
            eng.wait_ge(used, i * per_turn(name)[0] + (PLAN[name][0] + s + 1 + SRING))

        def wait_evac(eng, name, i, j):
            t = PLAN[name][1] + j
            eng.wait_ge(evac[t % 4], i * per_turn(name)[1] + (t // 4 + 2))

        def bank_of(name, j):
            return bank[(PLAN[name][1] + j) % 4]

        def evac_of(name, j):
            return evac[(PLAN[name][1] + j) % 4]

        block = ctx.enter_context(nc.Block())

        @block.sync
        def _(sp):
            def load(base, i, s):
                p = base + s
                sp.wait_ge(lo_done, i * 8 + (p + 1))
                src = stream[p] if isinstance(i, int) else stream[ds(i * 8 + p, 1)].rearrange("a p c -> p (a c)")
                sp.dma_start(raw[:, p % RING, :], src).then_inc(raw_landed[p % RING], 16)

            def load_run(base, n):
                whole = n // 8 * 8 if n >= 16 else 0
                if whole:
                    with sp.Fori(0, whole // 8) as i:
                        for s in range(8):
                            load(base, i, s)
                for s in range(whole, n):
                    load(base + s, 0, 0)

            def ada_run(gu, mod0, turns):
                base = PLAN[gu][0] + 8
                with sp.Fori(0, turns) as i:
                    for s in range(8):
                        load(base, i, s)
                        if s == 0 and mod0 == 0:
                            sp.wait_ge(used, PLAN[gu][0] + 1 + SRING)
                        sp.wait_ge(ada_used, i * 8 + (8 * mod0 + s + 1))
                        sp.dma_start(ADA[:, s % 2, :], ada[ds(i * 8 + (8 * mod0 + s), 1)].rearrange(
                            "a p c -> p (a c)")).then_inc(ada_landed[s % 2], 16)

            a, b = PLAN["gu1a"][0] + 8, PLAN["gu1b"][0] + 8
            for s in ld_x:
                sp.wait_ge(s, 16)
            load_run(0, a)
            ada_run("gu1a", 0, 6)
            load_run(a + 48, b - a - 48)
            ada_run("gu1b", 6, 3)
            load_run(b + 24, NPANELS - b - 24)
            for k in range(KD):
                sp.wait_ge(x_ready, X_FINAL + k + 1)
                sp.dma_start(out[:, k, :], X[:, k, :]).then_inc(out_done, 16)
            sp.wait_ge(out_done, 16 * KD)

        @block.gpsimd
        def _(pool):
            def low(i, s):
                pool.wait_ge(hi_done, i * 8 + (s + 1))
                pool.tensor_tensor(wlo[:, s % SRING, :], raw[:, s % RING, :], whi[:, s % SRING, :].bitcast(F32),
                                   ALU.subtract).then_inc(lo_done, 1)

            def low_run(lo, hi):
                n = (hi - lo) // 8
                if n:
                    with pool.Fori(0, n) as i:
                        for s in range(8):
                            low(i, lo + s)
                for s in range(lo + 8 * n, hi):
                    low(0, s)

            def add_pairs(norm):
                for j in range(4):
                    pool.wait_ge(sq_ready, 8 * norm + 2 * j + 2)
                    pool.tensor_tensor(PAIRS[:, j, :], SQ8[:, 2 * j, :], SQ8[:, 2 * j + 1, :], ALU.add)\
                        .then_inc(pair_ready, 1)

            def add_up(norm, k):
                pool.wait_ge(sq_ready, 8 * norm + k + 1)
                if k == 1:
                    pool.tensor_tensor(SQ_ACC, sq[:, 0, :], sq[:, 1, :], ALU.add).then_inc(sq_summed, 2)
                else:
                    pool.wait_ge(sq_summed, 8 * norm + k)
                    pool.tensor_tensor(SQ_ACC, SQ_ACC, sq[:, k % 2, :], ALU.add).then_inc(sq_summed, 1)

            pool.wait_ge(const_ready, 1)
            at = 0
            for norm, stage, K in (("n1", "win", 0), ("n2", "mix", KD), ("post1", "dn2b", FB), ("pre2", "qka", 0),
                                   ("post2", "wout", KD),
                                   ("pre3", "gu3a", 0), ("post3", "dn3b", FB)):
                if K:
                    for k in range(1, KD - 1):
                        to = min(PLAN[stage][0] + ((k + 1) * K - 1) // 4 + 1 + AHEAD, NPANELS)
                        low_run(at, to)
                        add_up(NORM[norm], k)
                        at = to
                else:
                    to = PLAN[stage][0] + (AHEAD if at else 0)
                    low_run(at, to)
                    add_pairs(NORM[norm])
                    at = to
                if stage == "win":
                    for k in range(1, KD - 1):
                        to = PLAN[stage][0] + 8 * (k + 4)
                        low_run(at, to)
                        at = to
                        pool.wait_ge(conv_done, k + 1)
                        if k > 1:
                            pool.wait_ge(conv_added, k - 1)
                        pool.tensor_tensor(SQ_ACC, U[:, 0, PAD:U_ST] if k == 1 else SQ_ACC, U[:, k, PAD:U_ST], ALU.add)\
                            .then_inc(conv_added, 1)
            low_run(at, NPANELS)

        @block.scalar
        def _(act):
            own = Steps(act, achain)

            def split(name, i, s):
                p = PLAN[name][0] + s
                if isinstance(i, int) and p + 8 * i >= NPANELS:
                    return
                n = per_turn(name)[0]
                act.wait_ge(raw_landed[p % RING], i * (16 * n // RING) + (p // RING + 1) * 16)
                act.wait_ge(used, i * n + (p + 1))
                act.activation(whi[:, p % SRING, :], raw[:, p % RING, :], ACT.Copy).then_inc(hi_done, 1)

            def tick(name, i, s, n=2):
                for x in range(s, s + n):
                    split(name, i, x + AHEAD)

            def square(norm, k, value):
                if 8 * norm + k - 1 > 0:
                    act.wait_ge(sq_summed, 8 * norm + k - 1)
                act.activation(sq[:, k % 2, :], value, ACT.Square).then_inc(sq_ready, 1)

            def pair_square(k, value):
                act.activation(SQ8[:, k, :], value, ACT.Square).then_inc(sq_ready, 1)

            def round_a(fill, val, shift=None):
                for k in range(KD):
                    act.wait_ge(a_val, val + k + 1)
                    if shift is None:
                        act.activation(a_hi[:, k, :], tmp[:, k % 2, :], ACT.Copy).then_inc(a_hi_w, 1)
                    else:
                        act.activation(a_hi[:, k, :], tmp[:, k % 2, :], ACT.Identity, bias=shift(k)).then_inc(a_hi_w, 1)

            def packed_tick(name, m, K):
                lo, hi = -(-m * K // 4), -(-(m + 1) * K // 4)
                tick(name, 0, lo, hi - lo)

            def wide_tick(name, i, j):
                tick(name, i, *((0, 5) if j == 0 else (4 + j, 1)))

            def ffn_gates(name, turns):
                with act.Fori(0, turns) as i:
                    for pr in range(2):
                        wide_tick(name, i, 2 * pr)
                        wait_used(act, name, i, 4 + 2 * pr)
                        wait_evac(act, name, i, 2 * pr + 1 - 4)
                        act.activation(SIL[:, pr, :], bank_of(name, 2 * pr)[:, :], ACT.Silu)\
                           .then_inc(evac_of(name, 2 * pr), 1)
                        wide_tick(name, i, 2 * pr + 1)
                        wait_evac(act, name, i, 2 * pr + 1)
                        act.activation(b_hi[:, ds(i * 2 + pr, 1), :].rearrange("p a t -> p (a t)"), tmp[:, pr, :],
                                       ACT.Copy).then_inc(b_hi_w, 1)

            def ffn_down(name, K, norm, copy):
                for m in range(KD):
                    packed_tick(name, m, K)
                    if copy:
                        wait_used(act, name, 0, ((m + 1) * K - 1) // 4)
                        act.activation(Y[:, m, :], bank_of(name, m)[:, :], ACT.Copy).then_inc(evac_of(name, m), 1)
                    if norm is not None:
                        wait_evac(act, name, 0, m)
                        square(norm, m, (X if norm in (NORM["n2"], NORM["nf"]) else Y)[:, m, :])

            def ffn(n, norm):
                ffn_gates(f"gu{n}a", FA // 2)
                ffn_down(f"dn{n}a", FA, None, n > 1)
                ffn_gates(f"gu{n}b", FB // 2)
                ffn_down(f"dn{n}b", FB, norm, False)

            for j in range(4):
                act.dma_start(X[:, 2 * j:2 * j + 2, :], xT[:, 2 * j:2 * j + 2, :]).then_inc(ld_x[j], 16)
            act.dma_start(consts[:, :, :], consts_d).then_inc(ld_c, 16)
            act.dma_start(cols[:, :], cols_d).then_inc(ld_c, 16)
            act.dma_start(G[:, 0:8 * P], masks_d.rearrange("p a b -> p (a b)")).then_inc(ld_m, 16)
            act.wait_ge(const_ready, 1)
            for k in range(KD):
                if k % 2 == 0:
                    act.wait_ge(ld_x[k // 2], 16)
                pair_square(k, X[:, k, :])
            act.wait_ge(ld_c, 32)
            own.next(act.activation(lru_t[:, 0, :], cols[:, COLS["lru_lambda"][0]:COLS["lru_lambda"][0] + KR], ACT.Abs))
            act.activation(lru_t[:, 1, :], lru_t[:, 0, :], ACT.Exp, scale=-1.0).then_inc(lam_e, 1)
            act.activation(small[:, 7, 0:8], cols[:, COLS["c_2"][0]:COLS["c_2"][0] + 8], ACT.Silu).then_inc(silc, 1)
            for s in range(AHEAD):
                split("win", 0, s)
            round_a("h1", 0)

            with act.Fori(0, 4) as i:
                for pr in range(2):
                    for j in range(2 * pr, 2 * pr + 2):
                        wide_tick("win", i, j)
                    wait_used(act, "win", i, 5 + 2 * pr)
                    wait_evac(act, "win", i, 2 * pr - 4)
                    act.activation(R5[:, pr, :], bank[2 * pr + 1][:, :], ACT.Sigmoid,
                                   bias=cols[:, ds(i * 4 + (COLS["b_in"][0] + 2 * pr + 1), 1)])\
                       .then_inc(evac[2 * pr + 1], 1)
            for t in range(16, 16 + 2 * KR):
                m = (t - 16) % KR
                wide_tick("win", t // 4, t % 4)
                wait_used(act, "win", t // 4, 4 + t % 4)
                act.activation(XR[:, m + 1, LPAD:X_ST] if t < 16 + KR else RG[:, m, :], bank[t % 4][:, :],
                               ACT.Identity if t < 16 + KR else ACT.Gelu_apprx_tanh, bias=col("b_in", t))\
                   .then_inc(evac[t % 4], 1)
            wait_evac(act, "win", 0, 12)
            wait_evac(act, "win", 0, 14)
            for m in range(2 * KD):
                t = 16 + 2 * KR + m
                if t == 48:
                    for k in range(KD):
                        if k % 2 == 0:
                            tick("win", 12, k // 2, 1)
                        act.wait_ge(centred, k + 1)
                        square(NORM["ln"], k, U[:, k, PAD:U_ST])
                    tick("win", 12, 4, 1)
                else:
                    wide_tick("win", t // 4, t % 4)
                wait_used(act, "win", t // 4, 4 + t % 4)
                if m >= 2:
                    act.wait_ge(stage_out[m % 2], 16 * (m // 2))
                act.activation(STG[:, m % 2, :], bank[t % 4][:, :], ACT.Sigmoid, bias=col("b_in", t))\
                   .then_inc(evac[t % 4], 1)
                wait_evac(act, "win", 0, t)
                act.dma_start((spill_ga if m < KD else spill_gb)[:, m % KD, :], STG[:, m % 2, :])\
                   .then_inc(stage_out[m % 2], 16)
            for j in range(2):
                act.wait_ge(stage_out[j], 16 * KD)

            def lru_gates(half, some=range(5)):
                name = f"gates{half}"
                for m in some:
                    if half:
                        act.wait_ge(lru_done, m + 1)
                    for w in range(2):
                        o = 2 * m + w
                        tick(name, 0, o, 1)
                        wait_used(act, name, 0, o)
                        n = 5 * half + m
                        if w and n >= 2:
                            act.wait_ge(ix_done, n - 1)
                        act.activation(R5[:, m, :] if w == 0 else IG[:, n % 2, :], bank_of(name, o)[:, :], ACT.Sigmoid,
                                       bias=col("lru_bx" if w else "lru_ba", n)).then_inc(evac_of(name, o), 1)

            def lru_decay(half):
                for m in range(5):
                    n = 5 * half + m
                    wait_evac(act, f"gates{half}", 0, 2 * m)
                    act.activation(A5[m], R5[:, m, :], ACT.Exp, scale=lru_c[:, 0, n:n + 1]).then_inc(achain, 1)
                    own.n += 1
                    act.wait_ge(achain, own.n)
                    act.activation(R5[:, m, :], R5[:, m, :], ACT.Tanh, scale=lru_c[:, 1, n:n + 1]).then_inc(decay, 1)

            def lru_root(half):
                for m in range(5):
                    act.wait_ge(var_ready, 5 * half + m + 1)
                    act.activation(R5[:, m, :], R5[:, m, :], ACT.Sqrt).then_inc(root, 1)

            for k in range(KD):
                act.wait_ge(a_val, 8 + k + 1)
                act.activation(tmp[:, k % 2, :], tmp[:, k % 2, :], ACT.Silu, bias=col("conv_ln_b", k)).then_inc(u_silu, 1)
                if k in (1, 3, 5):
                    lru_gates(0, (k // 2,))
            act.dma_start(GA[:, :, :], spill_ga).then_inc(ld_ga, 16)
            lru_gates(0, (3, 4))
            lru_decay(0)
            tick("convo0", 0, 0)
            tick("convo0", 0, 2)
            lru_root(0)
            tick("convo0", 0, 4)
            tick("convo0", 0, 6)
            lru_gates(1)
            lru_decay(1)
            tick("convo1", 0, 0)
            tick("convo1", 0, 2)
            lru_root(1)
            tick("convo1", 0, 4)
            tick("convo1", 0, 6)
            act.wait_ge(opb, FILL_B["yb"] + KR)
            act.dma_start(GB[:, :, :], spill_gb).then_inc(ld_gb, 16)
            act.dma_start(X[:, :, :], xT).then_inc(ld_x2, 16)
            for m in range(KD):
                packed_tick("lruo", m, KR)
                act.wait_ge(a_val, 16 + m + 1)
                act.activation(a_hi[:, m, :], tmp[:, m % 2, :], ACT.Copy).then_inc(a_hi_w, 1)
            for m in range(KD):
                tick("mix", 0, 2 * m)
                wait_evac(act, "mix", 0, m)
                square(NORM["n2"], m, X[:, m, :])
            round_a("hf1", 24)
            ffn(1, NORM["nf"])
            round_a("hf2", 32, lambda k: mods[:, k:k + 1])
            ffn(2, NORM["post1"])
            for k in range(KD):
                act.wait_ge(x_ready, KD + k + 1)
                pair_square(k, X[:, k, :])

            round_a("hmix2", 40, lambda k: mods[:, 24 + k:25 + k])
            for t in range(8):
                wide_tick("qka", t // 4, t % 4)
                wait_used(act, "qka", t // 4, 4 + t % 4)
                act.activation(QK[:, t % 4 * 2 + t // 4, :], bank_of("qka", t)[:, :], ACT.Copy,
                               scale=float(P) ** -0.5 if t < 4 else 1.0).then_inc(evac_of("qka", t), 1)
            act.dma_start(wa2, wa2_d).then_inc(ld_w2, 16)
            tick("low", 0, 0)
            wait_used(act, "low", 0, 1)
            act.activation(LOW[0:16, :], AUX[0:16, :], ACT.Copy).then_inc(low_out, 1)
            act.activation(LOW[32:48, :], AUX[32:48, :], ACT.Identity, bias=cols[32:48, COLS["b_f_2"][0]:NCOLS])\
               .then_inc(low_out, 1)

            def softplus_step(func, scale, bias):
                for h in range(5):
                    rows = slice(0, P) if h < 4 else slice(32, 48)
                    src = LT[rows, h, :] if func != ACT.Abs else (LA[rows, h, :] if h < 4 else LOW[rows, :])
                    if func == ACT.Ln:
                        act.activation(LT[rows, h, :], src, func, scale=scale, bias=bias).then_inc(la_ln, 1)
                    else:
                        own.next(act.activation(LT[rows, h, :], src, func, scale=scale))

            for i in range(2):
                for s in range(8):
                    tick("va", i, s, 1)
                    if i == 0 and s < GLA_HEADS:
                        act.wait_ge(la_psum, s + 1)
                        act.activation(LA[:, s, :], bank[4 + s][:, :], ACT.Identity, bias=col("b_a_2", s)).then_inc(la_z, 1)
                    if i == 0 and s == 4:
                        act.wait_ge(la_z, GLA_HEADS)
                        act.wait_ge(low_out, 2)
                        softplus_step(ACT.Abs, 1.0, 0.0)
                    if i == 0 and s == 6:
                        softplus_step(ACT.Exp, -1.0, 0.0)
                    if i == 1 and s == 2:
                        softplus_step(ACT.Ln, 1.0, 1.0)
                wait_used(act, "va", i, 7)
                for t in range(4):
                    act.activation(VA[:, t, i * SOME:(i + 1) * SOME], bank_of("va", t)[:, :], ACT.Copy)\
                       .then_inc(evac_of("va", t), 1)

            act.wait_ge(f_split, 1)
            act.dma_start(FHL[48:64, :].bitcast(F32), FLO.bitcast(F32)).then_inc(ld_f, 16)

            with act.Fori(0, GLA_HEADS) as i:
                def wait_in(what):
                    act.wait_ge(gla_in, i * len(GLA_IN) + (GLA_IN.index(what) + 2))

                def wait_mm(what):
                    act.wait_ge(gla_mm, i * len(GLA_MM) + (GLA_MM.index(what) + 2))

                def keep_rows(t):
                    wait_used(act, "rv", i, 7 if t < 4 else 2 * t + 1)
                    act.wait_ge(rows_out[t % 2], i * 64 + 16 * (t // 2 + 1))
                    act.activation(tmp[:, t % 2, :], bank_of("rv", t)[:, :], ACT.Copy).then_inc(evac_of("rv", t), 1)
                    wait_evac(act, "rv", i, t)
                    place = i * 4 + (t if t < 4 else 12 + t)
                    act.dma_start(spill_rv[:, ds(place, 1), :].rearrange("p a t -> p (a t)"), tmp[:, t % 2, :])\
                       .then_inc(rows_out[t % 2], 16)

                for label in GLA_EXP:
                    kind, arg = label[:2], int(label[2:] or 0)
                    if kind == "eb":
                        wait_in("bc")
                        ins = act.activation(EB, BC, ACT.Exp, scale=1 / TAU)
                    elif kind in ("ef", "es"):
                        wait_in(f"d{arg}")
                        m = P >> arg
                        half = slice(0, m) if kind == "ef" else slice(m, 2 * m)
                        v = E2[arg % 2].rearrange("p (n m) -> p n m", m=2 * m)[:, :, half]
                        ins = act.activation(v, v, ACT.Exp, scale=-1 / TAU if kind == "ef" else 1 / TAU)
                    elif kind == "eo":
                        keep_rows(4)
                        wait_in("do")
                        ins = act.activation(E2[0], E2[0], ACT.Exp, scale=1 / TAU)
                    elif kind == "ao":
                        keep_rows(5)
                        keep_rows(6)
                        tick("rv", i, 14, 1)
                        keep_rows(7)
                        tick("rv", i, 15, 1)
                        wait_mm("o1")
                        ins = act.activation(AO[:, 3 * P:6 * P], bank[7][:, 0:3 * P], ACT.Copy)
                    else:
                        out_ps = bank[4 + arg // 2][:, arg % 2 * GLA_V:(arg % 2 + 1) * GLA_V]
                        if kind == "sq":
                            wait_mm(f"pv{arg // 2}")
                            ins = act.activation(ON[:, arg, :], out_ps, ACT.Square, accum_out=small[:, 5, arg:arg + 1])
                        else:
                            wait_in("y")
                            ins = act.activation(ONH[:, ds(i, 1), arg, :].rearrange("p a e -> p (a e)"), out_ps, ACT.Copy,
                                                 scale=small[:, 6, arg:arg + 1])
                    ins.then_inc(gla_exp, 1)
                    if kind == "es":
                        if arg in (5, 6):
                            keep_rows(2 * arg - 10)
                            keep_rows(2 * arg - 9)
                        tick("rv", i, 2 * arg - 2)
            for j in range(2):
                act.wait_ge(rows_out[j], 16 * (4 * GLA_HEADS + 1))
            for dst, at, landed in ((R2, 0, ld_r), (VB, 8, ld_v)):
                for g in range(2):
                    act.dma_start(dst[:, :, g * SOME:(g + 1) * SOME], spill_rv[:, at + 4 * g:at + 4 * g + 4, :])\
                       .then_inc(landed, 16)

            def keep_qk(i, j):
                act.activation(QF[:, j % 4, :], bank_of("qkb", j)[:, :], ACT.Copy,
                               scale=FOX_HD ** -0.5 if j % 2 == 0 else 1.0).then_inc(evac_of("qkb", j), 1)

            for j in range(4):
                tick("qkb", 0, 2 * j)
                wait_used(act, "qkb", 0, 2 * j + 1)
                keep_qk(0, j)
                if j == 1:
                    act.wait_ge(ld_r, 32)
                    for t in range(4):
                        act.activation(R2[:, t, :], R2[:, t, :], ACT.Silu).then_inc(r_silu, 1)
            for m in range(KD):
                act.wait_ge(b_val, m + 1)
                act.activation(b_hi[:, m, :], tmp[:, m % 2, :], ACT.Copy).then_inc(b_hi_w, 1)

            def fox_turn(i, next_qk):
                for u in range(17):
                    if u < 16:
                        n = (u % 4 + 1) * P
                        act.wait_ge(fox_m, i * 16 + (u + 1))
                        act.wait_ge(fox_t, i * 16 + (u + 1))
                        act.activation(PR[:, u % 2, 0:n], bank[6 + u % 2][:, 0:n], ACT.Exp,
                                       bias=small[:, 6, u % 4:u % 4 + 1], accum_out=small[:, 5, u % 4:u % 4 + 1])\
                           .then_inc(fox_p, 1)
                    if u:
                        w = u - 1
                        n = (w % 4 + 1) * P
                        act.wait_ge(fox_t, i * 16 + (w + 3))
                        act.wait_ge(fox_o, i * 16 + (w + 1))
                        act.activation(PT[:, w % 2, 0:n], bank[4 + w % 2][:, 0:n], ACT.Copy).then_inc(fox_pt, 1)
                    if next_qk and u < 16 and u % 2 == 0:
                        tick("qkb", i, 8 + u // 2, 1)
                    if next_qk and u in (9, 11):
                        keep_qk(i, 4 + u // 10)
                if next_qk:
                    for j in (6, 7):
                        wait_used(act, "qkb", i, 2 * j + 1)
                        keep_qk(i, j)

            with act.Fori(0, FOX_HEADS // 4 - 1) as i:
                fox_turn(i, True)
            fox_turn(FOX_HEADS // 4 - 1, False)
            act.wait_ge(fox_o, 4 * FOX_HEADS + 2)
            act.dma_start(GA2[:, :, :], spill_rv[:, 2 * KD:3 * KD, :]).then_inc(ld_ga, 16)
            act.dma_start(GB2[:, :, :], spill_rv[:, 3 * KD:4 * KD, :]).then_inc(ld_gb, 16)
            for m in range(KD):
                act.wait_ge(ob_t, m + 1)
                act.activation(a_hi[:, m, :], bank[6 + m % 2][:, :], ACT.Copy).then_inc(a_hi_w, 1)
            act.wait_ge(ld_ga, 32)
            for m in range(KD):
                tick("pa", 0, 2 * m)
                act.activation(GA2[:, m, :], GA2[:, m, :], ACT.Sigmoid).then_inc(gate2, 1)
            act.wait_ge(ld_gb, 32)
            for m in range(KD):
                act.activation(GB2[:, m, :], GB2[:, m, :], ACT.Sigmoid).then_inc(gate2, 1)
            for m in range(KD):
                tick("pb", 0, 2 * m)
                act.wait_ge(b_val, KD + m + 1)
                act.activation(b_hi[:, m, :], tmp[:, m % 2, :], ACT.Copy).then_inc(b_hi_w, 1)
            for m in range(KD):
                tick("wout", 0, 2 * m)
                wait_used(act, "wout", 0, 2 * m + 1)
                act.activation(Y[:, m, :], bank_of("wout", m)[:, :], ACT.Copy).then_inc(evac_of("wout", m), 1)
                wait_evac(act, "wout", 0, m)
                square(NORM["post2"], m, Y[:, m, :])
            for k in range(KD):
                act.wait_ge(x_ready, 2 * KD + k + 1)
                pair_square(k, X[:, k, :])
            round_a("hf3", 48, lambda k: mods[:, 48 + k:49 + k])
            ffn(3, NORM["post3"])

        @block.tensor
        def _(pe):
            def panel(name, i, s, ks, out_ps, ops, first, last, q0=0, done=True, ready=None):
                p = PLAN[name][0] + s
                pe.wait_ge(lo_done, i * per_turn(name)[0] + (p + 1 + RING))
                hi, lo = ops
                for q, k in enumerate(ks):
                    if ready:
                        pe.wait_ge(ready[0], ready[1] + k + 1)
                    c = slice((q0 + q) * P, (q0 + q + 1) * P)
                    w_hi, w_lo = whi[:, p % SRING, c], wlo[:, p % SRING, c]
                    pe.matmul(out_ps, w_hi, hi[:, k, :], start=first and q == 0, stop=False)
                    pe.matmul(out_ps, w_lo, hi[:, k, :], start=False, stop=False)
                    mm = pe.matmul(out_ps, w_hi, lo[:, k, :], start=False, stop=last and q == len(ks) - 1)
                if done:
                    mm.then_inc(used, 1)

            def bank_free(name, i, j):
                t = PLAN[name][1] + j
                pe.wait_ge(evac[t % 4], i * per_turn(name)[1] + (t // 4 + 1))

            OPA, OPB = (a_hi, a_lo), (b_hi, b_lo)

            def tile8(name, i, j, ops, ready, fill, wait_ops):
                bank_free(name, i, j)
                for h in range(2):
                    if wait_ops:
                        pe.wait_ge(ready, fill + 4 * h + 4)
                    panel(name, i, 2 * j + h, range(4 * h, 4 * h + 4), bank_of(name, j)[:, :], ops, h == 0, h == 1)

            def stage8(name, ops, ready, fill, turns):
                with pe.Fori(0, turns) as i:
                    for j in range(4):
                        tile8(name, i, j, ops, ready, fill, j == 0)

            def wide_turn(name, i, ops, ready, fill, halves=(0, 1), beside=None):
                for h in halves:
                    for j in range(4):
                        if h == 0:
                            bank_free(name, i, j)
                        panel(name, i, 4 * h + j, range(4 * h, 4 * h + 4), bank_of(name, j)[:, :], ops, h == 0, h == 1,
                              ready=(ready, fill) if j == 0 else None)
                        if beside:
                            beside(4 * h + j)

            def wide_stage(name, ops, ready, fill, turns):
                with pe.Fori(0, turns) as i:
                    wide_turn(name, i, ops, ready, fill)

            def tile_packed(name, m, K, ops, ready, fill):
                bank_free(name, 0, m)
                k = 0
                while k < K:
                    f = m * K + k
                    n = min(4 - f % 4, K - k)
                    if m == 0:
                        pe.wait_ge(ready, fill + k + n)
                    panel(name, 0, f // 4, range(k, k + n), bank_of(name, m)[:, :], ops, k == 0, k + n == K,
                          q0=f % 4, done=(f + n) % 4 == 0)
                    k += n

            def sum_tile(k, value, done):
                for tt in range(4):
                    mm = pe.matmul(AUX[:, tt:tt + 1], value[:, tt * P:(tt + 1) * P], ones[:, 0:1],
                                   start=(k == 0 and tt == 0), stop=(k == KD - 1 and tt == 3), skip_group_check=True)
                if done is not None:
                    mm.then_inc(done, 1)

            def sum_up(norm):
                pe.wait_ge(sq_summed, 8 * norm + KD - 1)
                sum_tile(0, SQ_ACC, None)
                sum_square(norm, KD - 1)

            def sum_square(norm, k):
                pe.wait_ge(sq_ready, 8 * norm + k + 1)
                sum_tile(k, sq[:, k % 2, :], sq_summed)

            def sum_pairs(n, norm):
                for j in range(4):
                    pe.wait_ge(pair_ready, 4 * n + j + 1)
                    for tt in range(4):
                        mm = pe.matmul(AUX[:, tt:tt + 1], PAIRS[:, j, tt * P:(tt + 1) * P], ones[:, 0:1],
                                       start=(j == 0 and tt == 0), stop=(j == 3 and tt == 3), skip_group_check=True)
                    mm.then_inc(sq_summed, 2)

            def sum_both(k):
                pe.wait_ge(sq_ready, 8 * NORM["nf"] + k + 1)
                for tt in range(4):
                    mm = pe.matmul(AUX[:, 2 * tt:2 * tt + 2], sq[:, k % 2, tt * P:(tt + 1) * P], one_g2[:, k, :],
                                   start=(k == 0 and tt == 0), stop=(k == KD - 1 and tt == 3), skip_group_check=True)
                mm.then_inc(sq_summed, 1)

            def broadcast(n, src=tmp[:, 0, :], dst=BCAST):
                pe.wait_ge(st_ready, n)
                pe.matmul(dst[:, :], ones[:, :], src, start=True, stop=True).then_inc(bc_ready, 1)

            def ffn(n, norm, ada_mods, fill):
                for half, K in (("a", FA), ("b", FB)):
                    name = f"gu{n}{half}"
                    turns = K // 2
                    with_ada = 0 if not ada_mods else (6 if half == "a" else 3)
                    if with_ada:
                        with pe.Fori(0, with_ada) as i:
                            wide_turn(name, i, OPA, opa, fill)
                            m0 = 0 if half == "a" else 6
                            pe.wait_ge(ada_used, i * 8 + (8 * m0 + 8 + 2))
                            for j in range(8):
                                mm = pe.matmul(AUX[:, 8 + j:9 + j], ADA_ACC[:, j * P:(j + 1) * P], ones[:, 0:1],
                                               start=(j == 0), stop=(j == 7), skip_group_check=True)
                            mm.then_inc(ada_psum, 1)
                    if turns > with_ada:
                        with pe.Fori(with_ada, turns) as i:
                            wide_turn(name, i, OPA, opa, fill)
                    name = f"dn{n}{half}"
                    for m in range(KD):
                        tile_packed(name, m, K, OPB, opb, FILL_B[f"ffn{n}{half}"])
                        if n == 1 and half == "b" and m:
                            sum_both(m - 1)
                if n == 1:
                    sum_both(KD - 1)
                else:
                    sum_up(norm)

            pe.wait_ge(const_ready, 1)
            sum_pairs(0, "n1")
            broadcast(1)
            wide_stage("win", OPA, opa, FILL_A["h1"], 9)

            def win_turn(i, halves=(0, 1), beside=None):
                wide_turn("win", i, OPA, opa, FILL_A["h1"], halves, beside)

            def sum_two(s):
                for k in (2 * s, 2 * s + 1):
                    if k < KD:
                        sum_square(NORM["ln"], k)
                if s == 5:
                    broadcast(3)

            win_turn(9)
            win_turn(10)
            pe.wait_ge(conv_added, KD - 2)
            sum_tile(0, SQ_ACC, None)
            pe.wait_ge(conv_done, KD)
            sum_tile(KD - 1, U[:, KD - 1, PAD:U_ST], mean_summed)
            win_turn(11, (0,))
            broadcast(2)
            win_turn(11, (1,))
            win_turn(12, beside=sum_two)

            def lru_gates(half):
                name = f"gates{half}"
                for o in range(10):
                    m = o // 2
                    ks = [k for k in (m - 1, m, m + 1) if 0 <= k < 5]
                    bank_free(name, 0, o)
                    pe.wait_ge(opb, FILL_B["xb"] + 5 * half + ks[-1] + 1)
                    panel(name, 0, o, [5 * half + k for k in ks], bank_of(name, o)[:, :], OPB, True, True,
                          q0=ks[0] - m + 1)

            lru_gates(0)
            for m in range(4):
                tile8("convo0", 0, m, OPA, opa, FILL_A["u2"], m == 0)
            lru_gates(1)
            for m in range(4):
                tile8("convo1", 0, m, OPA, opa, FILL_A["u2"], False)
            for m in range(KD):
                tile_packed("lruo", m, KR, OPB, opb, FILL_B["yb"])
            for m in range(KD):
                tile8("mix", 0, m, OPA, opa, FILL_A["mix"], m == 0)
            sum_up(NORM["n2"])
            broadcast(4)
            ffn(1, NORM["nf"], True, FILL_A["hf1"])
            broadcast(5)
            broadcast(6, src=sq[:, 0, :], dst=bank[6])
            ffn(2, NORM["post1"], False, FILL_A["hf2"])
            broadcast(7)
            sum_pairs(1, "pre2")
            broadcast(8)

            def row_panel(name, i, k, ops):
                hi, lo = ops
                p = PLAN[name][0] + k
                pe.wait_ge(lo_done, i * per_turn(name)[0] + (p + 1 + RING))
                for j in range(4):
                    if k == 0:
                        bank_free(name, i, j)
                    c = slice(j * P, (j + 1) * P)
                    out_ps = bank_of(name, j)[:, :]
                    w_hi, w_lo = whi[:, p % SRING, :], wlo[:, p % SRING, :]
                    pe.matmul(out_ps, hi[:, k, c], w_hi, start=k == 0, stop=False)
                    pe.matmul(out_ps, hi[:, k, c], w_lo, start=False, stop=False)
                    mm = pe.matmul(out_ps, lo[:, k, c], w_hi, start=False, stop=k == KD - 1)
                mm.then_inc(used, 1)

            fill = FILL_A["hmix2"]
            wide_stage("qka", OPA, opa, fill, 2)
            for h in range(2):
                panel("low", 0, h, range(4 * h, 4 * h + 4), AUX[:, :], OPA, h == 0, h == 1)
            pe.wait_ge(low_out, 2)
            pe.wait_ge(ld_w2, 16)
            for h in range(GLA_HEADS):
                pe.matmul(bank[4 + h][:, :], wa2[:, h * P:(h + 1) * P], LOW[0:16, :], start=True, stop=True)\
                  .then_inc(la_psum, 1)
            for i in range(2):
                for k in range(KD):
                    row_panel("va", i, k, OPA)
            pe.wait_ge(la_z, GLA_HEADS)

            with pe.Fori(0, GLA_HEADS) as i:
                def wait_in(what):
                    pe.wait_ge(gla_in, i * len(GLA_IN) + (GLA_IN.index(what) + 2))

                def beside(l):
                    if l < 4:
                        row_panel("rv", i, 2 * l, OPA)
                        row_panel("rv", i, 2 * l + 1, OPA)
                    else:
                        tile8("gab", i, l - 4, OPA, opa, fill, False)

                def wait_cp(what):
                    pe.wait_ge(gla_cp, i * len(GLA_CP) + (GLA_CP.index(what) + 2))

                def wait_exp(what):
                    pe.wait_ge(gla_exp, i * len(GLA_EXP) + (GLA_EXP.index(what) + 2))

                q_h = QK[:, ds(i * 2, 1), :].rearrange("p a t -> p (a t)")
                beside(0)
                wait_in("kc")
                for c in range(4):
                    cc = slice(c * P, (c + 1) * P)
                    mm = pe.matmul(bank[6][:, cc], KC[:, cc], q_h[:, cc], start=True, stop=True)
                mm.then_inc(gla_mm, 1)
                for l in range(1, 8):
                    wait_in(f"q{l}")
                    if l >= 2:
                        wait_cp(f"c{l - 2}")
                    for c in range(4):
                        cc = slice(c * P, (c + 1) * P)
                        mm = pe.matmul(bank[6 + l % 2][:, cc], KQ[:, cc], KQ[:, cc], start=True, stop=True)
                    mm.then_inc(gla_mm, 1)
                    beside(l)
                wait_cp("c6")
                wait_in("kd")
                pe.matmul(bank[6][:, 0:3 * P], KQ[:, 0:P], QX[:, 0:3 * P], start=True, stop=True).then_inc(gla_mm, 1)
                wait_cp("c7")
                pe.matmul(bank[7][:, 0:2 * P], KQ[:, P:2 * P], QX[:, 3 * P:5 * P], start=True, stop=True)
                pe.matmul(bank[7][:, 2 * P:3 * P], KQ[:, 2 * P:3 * P], QX[:, 5 * P:6 * P], start=True, stop=True)\
                  .then_inc(gla_mm, 1)
                wait_cp("ao")
                wait_exp("ao")
                place = {(0, 1): 0, (0, 2): 1, (0, 3): 2, (1, 2): 3, (1, 3): 4, (2, 3): 5}
                for t in range(4):
                    out_ps = bank[4 + t // 2][:, t % 2 * GLA_V:(t % 2 + 1) * GLA_V]
                    for j in range(t + 1):
                        a = AD[:, t * P:(t + 1) * P] if j == t else AO[:, place[j, t] * P:(place[j, t] + 1) * P]
                        mm = pe.matmul(out_ps, a, VA[:, j, ds(i * GLA_V, GLA_V)], start=j == 0, stop=j == t)
                    if t % 2:
                        mm.then_inc(gla_mm, 1)

            for j in range(4):
                tile8("qkb", 0, j, OPA, opa, fill, False)
            pe.wait_ge(r_prod, 2 * GLA_HEADS)
            for m in range(KD):
                if m >= 2:
                    pe.wait_ge(b_val, m - 1)
                for t in range(4):
                    mm = pe.transpose(bank[6 + m % 2][:, t * P:(t + 1) * P],
                                      ONH[:, m // 2, t, m % 2 * P:(m % 2 + 1) * P], ident)
                mm.then_inc(oa_t, 1)
            pe.wait_ge(ld_v, 32)

            def fox_turn(i, next_qk):
                def scores(u):
                    h, t = u // 4, u % 4
                    n = (t + 1) * P
                    r = slice(FOX_HD * (h % 2), FOX_HD * (h % 2 + 1))
                    s_ps = bank[6 + u % 2][:, 0:n]
                    pe.wait_ge(fox_p, i * 16 + (u + 1))
                    if t == 0:
                        pe.wait_ge(fox_nf, i * 4 + (h + 1))
                        wait_evac(pe, "qkb", i, h // 2 * 2)
                        wait_evac(pe, "qkb", i, h // 2 * 2 + 1)
                    pe.matmul(s_ps, QF[r, 2 * (h // 2), t * P:(t + 1) * P], QF[r, 2 * (h // 2) + 1, 0:n],
                              start=True, stop=False)
                    pe.matmul(s_ps, ONES_R[32:64, :], NFH[32:64, h % 2, 0:n], start=False, stop=True)\
                      .then_inc(fox_s, 1)

                scores(0)
                scores(1)
                for u in range(16):
                    h, t = u // 4, u % 4
                    pe.wait_ge(fox_p, i * 16 + (u + 3))
                    pe.wait_ge(fox_out, i * 16 + (u + 1))
                    for j in range(t + 1):
                        c = slice(j * P, (j + 1) * P)
                        mm = pe.transpose(bank[4 + u % 2][:, c], PR[:, u % 2, c], ident)
                    mm.then_inc(fox_t, 1)
                    if u < 14:
                        scores(u + 2)
                    if next_qk:
                        j = 4 + u // 4
                        if u % 4 == 0:
                            bank_free("qkb", i, j)
                        k = 2 * (u % 4)
                        panel("qkb", i, 8 + u // 2, (k, k + 1), bank_of("qkb", j)[:, :], OPA, u % 4 == 0, u % 4 == 3,
                              q0=k % 4, done=u % 2 == 1)
                    pe.wait_ge(fox_pt, i * 16 + (u + 3))
                    for j in range(t + 1):
                        mm = pe.matmul(bank[4 + u % 2][:, 0:FOX_HD], PT[:, u % 2, j * P:(j + 1) * P],
                                       VB[:, j, ds(i * (4 * FOX_HD) + h * FOX_HD, FOX_HD)],
                                       start=j == 0, stop=j == t)
                    mm.then_inc(fox_o, 1)

            with pe.Fori(0, FOX_HEADS // 4 - 1) as i:
                fox_turn(i, True)
            fox_turn(FOX_HEADS // 4 - 1, False)
            pe.wait_ge(fox_out, 64 + 2)
            for m in range(KD):
                if m >= 2:
                    pe.wait_ge(opa, FILL_A["ob"] + m - 1)
                else:
                    pe.wait_ge(opb, FILL_B["oa"] + KD)
                for t in range(4):
                    mm = pe.transpose(bank[6 + m % 2][:, t * P:(t + 1) * P], OB[:, t, m * P:(m + 1) * P], ident)
                mm.then_inc(ob_t, 1)
            stage8("pa", OPB, opb, FILL_B["oa"], 2)
            stage8("pb", OPA, opa, FILL_A["ob"], 2)
            for m in range(KD):
                tile8("wout", 0, m, OPB, opb, FILL_B["merged"], m == 0)
            sum_up(NORM["post2"])
            broadcast(9)
            sum_pairs(2, "pre3")
            broadcast(10)
            ffn(3, NORM["post3"], False, FILL_A["hf3"])
            broadcast(11)

        @block.vector
        def _(dve):
            own = Steps(dve, vchain)
            stat = [0]
            filled = {"a": 0, "b": 0}

            def settle():
                for s, n in ((opa, filled["a"]), (opb, filled["b"])):
                    if n:
                        dve.wait_ge(s, n)

            def rsqrt(value, n, scale):
                v, y, a, b = (small[:, r, 0:n] for r in range(4))
                own.next(dve.tensor_scalar(v, value, scale, EPS, ALU.mult, ALU.add))
                own.next(dve.tensor_scalar(y.bitcast(I32), v.bitcast(I32), -0.5, float(0x5F3759DF), ALU.mult, ALU.add))
                for _ in range(3):
                    own.next(dve.tensor_tensor(a, y, y, ALU.mult))
                    own.next(dve.scalar_tensor_tensor(out=b, in0=a, scalar=-0.5, in1=v, op0=ALU.mult, op1=ALU.mult))
                    own.next(dve.scalar_tensor_tensor(out=y, in0=b, scalar=1.5, in1=y, op0=ALU.add, op1=ALU.mult))

            RSQRT_STEPS = 11

            def diagonal(y, dst=tmp[:, 0, :]):
                settle()
                dve.tensor_tensor(dst.rearrange("p (j t) -> p j t", t=P),
                                  consts[:, 0:1, :].to_broadcast([P, 4, P]),
                                  y[:, 0:4].rearrange("p (j o) -> p j o", o=1).to_broadcast([P, 4, P]), ALU.mult)\
                   .then_inc(st_ready, 1)
                stat[0] += 1

            def norm_stat(norm):
                dve.wait_ge(sq_summed, 8 * (norm + 1))
                rsqrt(AUX[:, 0:4], 4, 1.0 / D)
                diagonal(small[:, 1, :])
                dve.wait_ge(bc_ready, stat[0])

            def lo_a(fill, k, shift=None):
                dve.wait_ge(a_hi_w, FILL_A[fill] + k + 1)
                if shift is None:
                    ins = dve.tensor_tensor(a_lo[:, k, :], tmp[:, k % 2, :], a_hi[:, k, :].bitcast(F32), ALU.subtract)
                else:
                    ins = dve.scalar_tensor_tensor(out=a_lo[:, k, :], in0=tmp[:, k % 2, :], scalar=shift(k),
                                                   in1=a_hi[:, k, :].bitcast(F32), op0=ALU.add, op1=ALU.subtract)
                ins.then_inc(opa, 1)

            def operand_a(fill, scale, shift=None):
                for k in range(KD + 1):
                    if k < KD:
                        if k > 1:
                            dve.wait_ge(opa, FILL_A[fill] + k - 1)
                        dve.scalar_tensor_tensor(out=tmp[:, k % 2, :], in0=X[:, k, :], scalar=scale(k), in1=BCAST[:, :],
                                                 op0=ALU.mult, op1=ALU.mult).then_inc(a_val, 1)
                    if k:
                        lo_a(fill, k - 1, shift)
                filled["a"] = FILL_A[fill] + KD

            def ada_block(i, mod0, s):
                dve.wait_ge(ada_landed[s % 2], i * 64 + (64 * mod0 + 16 * (s // 2 + 1)))
                c = small[:, 7, s:s + 1]
                if s == 0:
                    ins = dve.tensor_scalar(ADA_ACC, ADA[:, 0, :], c, None, ALU.mult)
                else:
                    ins = dve.scalar_tensor_tensor(out=ADA_ACC, in0=ADA[:, s % 2, :], scalar=c, in1=ADA_ACC,
                                                   op0=ALU.mult, op1=ALU.add)
                ins.then_inc(ada_used, 1)
                dve.wait_ge(ada_used, i * 8 + (8 * mod0 + s + 3))

            def gate_pair(name, i, pr, at):
                wait_evac(dve, name, i, 2 * pr)
                wait_used(dve, name, i, 5 + 2 * pr)
                dve.wait_ge(opb, i * 2 + (at + pr - 1))
                dve.tensor_tensor(tmp[:, pr, :], SIL[:, pr, :], bank_of(name, 2 * pr + 1)[:, :], ALU.mult)\
                   .then_inc(evac_of(name, 2 * pr + 1), 1)
                dve.wait_ge(b_hi_w, i * 2 + (at + pr + 1))
                dve.tensor_tensor(b_lo[:, ds(i * 2 + pr, 1), :].rearrange("p a t -> p (a t)"), tmp[:, pr, :],
                                  b_hi[:, ds(i * 2 + pr, 1), :].rearrange("p a t -> p (a t)").bitcast(F32),
                                  ALU.subtract).then_inc(opb, 1)

            def derive():
                for b in range(3):
                    own.next(dve.scalar_tensor_tensor(
                        out=derived[:, b, :], in0=mods[:, 24 * b + 8:24 * b + 16], scalar=1.0,
                        in1=cols[:, COLS["g_pre_2"][0] + 8 * b:COLS["g_pre_2"][0] + 8 * b + 8], op0=ALU.add, op1=ALU.mult))
                    own.next(dve.scalar_tensor_tensor(
                        out=derived[:, 3 + b, :], in0=mods[:, 24 * b + 16:24 * b + 24], scalar=1.0 if b == 1 else 0.5,
                        in1=cols[:, COLS["g_post_2"][0] + 8 * b:COLS["g_post_2"][0] + 8 * b + 8], op0=ALU.mult, op1=ALU.mult))
                own.next(dve.tensor_tensor(derived[:, 6, :], derived[:, 0, :],
                                           cols[:, COLS["norm_f_g"][0]:COLS["norm_f_g"][0] + KD], ALU.mult))

            def ffn(n, with_ada):
                for half, K in (("a", FA), ("b", FB)):
                    name = f"gu{n}{half}"
                    turns = K // 2
                    ada_turns = 0 if not with_ada else (6 if half == "a" else 3)
                    at = FILL_B[f"ffn{n}{half}"]
                    mod0 = 0 if half == "a" else 6
                    if ada_turns:
                        with dve.Fori(0, ada_turns) as i:
                            for pr in range(2):
                                for s in ((0, 1, 2, 3, 4, 5), (6, 7))[pr]:
                                    ada_block(i, mod0, s)
                                gate_pair(name, i, pr, at)
                            dve.wait_ge(ada_psum, i + (mod0 + 1))
                            own.begin(i, 1)
                            own.next(dve.tensor_tensor(mods[:, ds(i * 8 + 8 * mod0, 8)], AUX[:, 8:16],
                                                       cols[:, ds(i * 8 + (COLS["b_ada_2"][0] + 8 * mod0), 8)], ALU.add))
                            own.end(ada_turns)
                    if turns > ada_turns:
                        with dve.Fori(ada_turns, turns) as i:
                            for pr in range(2):
                                gate_pair(name, i, pr, at)
                    filled["b"] = at + K
                    name = f"dn{n}{half}"
                    if n == 1 and half == "b":
                        derive()
                    for m in range(KD):
                        if n > 1 and half == "a":
                            break
                        acc = X if n == 1 else Y
                        if n > 1:
                            wait_evac(dve, f"dn{n}a", 0, m)
                        wait_used(dve, name, 0, ((m + 1) * K - 1) // 4)
                        dve.tensor_tensor(acc[:, m, :], acc[:, m, :], bank_of(name, m)[:, :], ALU.add)\
                           .then_inc(evac_of(name, m), 1)

            dve.memset(ones[:, :], 1.0).then_inc(vchain, 1)
            own.n += 1
            dve.wait_ge(vchain, 1)
            for s, n in ((lo_done, RING), (used, SRING), (ada_used, 2)):
                dve.memset(small[:, 4, 0:1], 0.0).then_inc(s, n)
                dve.wait_ge(s, n)
            for s in evac:
                dve.memset(small[:, 4, 0:1], 0.0).then_inc(s, 1)
                dve.wait_ge(s, 1)
            dve.memset(small[:, 5, 0:1], 0.0).then_inc(const_ready, 1)
            dve.wait_ge(ld_c, 32)
            for s in ld_x:
                dve.wait_ge(s, 16)
            norm_stat(NORM["n1"])
            operand_a("h1", lambda k: col("norm1_g", k))
            own.next(dve.memset(one_g2[:, :, 0:1], 1.0))
            g = cols[:, COLS["norm_f_g"][0]:COLS["norm_f_g"][0] + KD]
            own.next(dve.tensor_tensor(one_g2[:, :, 1], g, g, ALU.mult))
            dve.wait_ge(ld_m, 16)
            own.next(dve.tensor_copy(masks[:, :, :].rearrange("p a b -> p (a b)"), G[:, 0:8 * P]))
            own.next(dve.memset(U[:, :, 0:PAD], 0.0))
            own.next(dve.memset(XR[:, :, 0:LPAD], 0.0))

            dve.wait_ge(lam_e, 1)
            w, w2, acc = (lru_t[:, r, :] for r in (0, 2, 3))
            e = lru_t[:, 1, :]
            own.next(dve.tensor_scalar(w2, e, 2.0, None, ALU.add))
            own.next(dve.reciprocal(acc, w2))
            own.next(dve.tensor_tensor(w, e, acc, ALU.mult))
            own.next(dve.tensor_tensor(w2, w, w, ALU.mult))
            own.next(dve.tensor_scalar(acc, w2, 1.0 / 17, 1.0 / 15, ALU.mult, ALU.add))
            for n in (13, 11, 9, 7, 5, 3, 1):
                own.next(dve.tensor_tensor(acc, acc, w2, ALU.mult))
                own.next(dve.tensor_scalar(acc, acc, 1.0 / n, None, ALU.add))
            own.next(dve.scalar_tensor_tensor(out=acc, in0=acc, scalar=2.0, in1=w, op0=ALU.mult, op1=ALU.mult))
            lam = cols[:, COLS["lru_lambda"][0]:COLS["lru_lambda"][0] + KR]
            own.next(dve.tensor_scalar(w, lam, -1.0, 0.0, ALU.mult, ALU.max))
            own.next(dve.tensor_tensor(w, w, acc, ALU.add))
            own.next(dve.tensor_scalar(lru_c[:, 0, :], w, -8.0, None, ALU.mult))
            own.next(dve.tensor_scalar(lru_c[:, 1, :], w, 8.0, None, ALU.mult))

            def conv_taps(m, lo, hi):
                dst = U[:, ds(m, 1), PAD:U_ST].rearrange("p a t -> p (a t)")
                for k in range(lo, hi):
                    src = U[:, ds(m + 1, 1), k:k + T].rearrange("p a t -> p (a t)")
                    wk = cols[:, ds(m + (COLS["conv_dw_w"][0] + 8 * k), 1)]
                    acc = tmp[:, 0, :] if k % 2 else dst
                    if k == 0:
                        ins = dve.tensor_scalar(dst, src, wk, cols[:, ds(m + COLS["conv_dw_b"][0], 1)],
                                                ALU.mult, ALU.add)
                    elif k == 1:
                        ins = dve.tensor_scalar(acc, src, wk, None, ALU.mult)
                    else:
                        ins = dve.scalar_tensor_tensor(out=acc, in0=src, scalar=wk, in1=acc, op0=ALU.mult, op1=ALU.add)
                    own.behind(ins)
                    if k == TAPS - 1:
                        own.all()
                        dve.tensor_tensor(dst, dst, tmp[:, 0, :], ALU.add).then_inc(conv_done, 1)
                        dve.wait_ge(conv_done, m + 1)

            with dve.Fori(0, 2) as i:
                own.begin(i, TAPS)
                for pr in range(4):
                    j = pr % 2
                    dve.wait_ge(evac[2 * j + 1], i * 2 + (pr // 2 + 2))
                    dve.scalar_tensor_tensor(
                        out=U[:, ds(i * 4 + (pr + 1), 1), PAD:U_ST].rearrange("p a t -> p (a t)"), in0=bank[2 * j][:, :],
                        scalar=cols[:, ds(i * 8 + (COLS["b_in"][0] + 2 * pr), 1)], in1=R5[:, j, :],
                        op0=ALU.add, op1=ALU.mult).then_inc(evac[2 * j], 1)
                    dve.wait_ge(evac[2 * j], i * 2 + (pr // 2 + 2))
                    conv_taps(i, 8 * pr, min(8 * pr + 8, TAPS))
                own.end(2)
            with dve.Fori(2, KD) as i:
                own.begin(i - 2, TAPS)
                conv_taps(i, 0, TAPS)
                own.end(KD - 2)
            def lru_conv(m):
                wait_evac(dve, "win", 0, 16 + m)
                dst = XR[:, m, LPAD:X_ST]
                for k in range(LTAPS):
                    src = XR[:, m + 1, k:k + T]
                    if k == 0:
                        ins = dve.tensor_scalar(dst, src, col("lru_conv_w", m), col("lru_conv_b", m), ALU.mult, ALU.add)
                    else:
                        ins = dve.scalar_tensor_tensor(out=dst, in0=src, scalar=col("lru_conv_w", KR * k + m), in1=dst,
                                                       op0=ALU.mult, op1=ALU.add)
                    own.next(ins)
                dve.tensor_copy(b_hi[:, m, :], dst).then_inc(b_hi_w, 1)
                dve.wait_ge(b_hi_w, m + 1)
                dve.tensor_tensor(b_lo[:, m, :], dst, b_hi[:, m, :].bitcast(F32), ALU.subtract).then_inc(opb, 1)

            for m in range(4):
                lru_conv(m)
            dve.wait_ge(mean_summed, 1)
            own.next(dve.tensor_scalar(small[:, 1, 0:4], AUX[:, 0:4], 1.0 / D, None, ALU.mult))
            diagonal(small[:, 1, :])
            lru_conv(4)
            lru_conv(5)
            dve.wait_ge(bc_ready, stat[0])
            for k in range(KD):
                dve.tensor_tensor(U[:, k, PAD:U_ST], U[:, k, PAD:U_ST], BCAST[:, :], ALU.subtract).then_inc(centred, 1)
            for m in range(6, KR):
                lru_conv(m)
            filled["b"] = FILL_B["yb"]

            def lru_input(half, some=range(5)):
                for m in some:
                    n = 5 * half + m
                    wait_evac(dve, f"gates{half}", 0, 2 * m + 1)
                    dve.tensor_tensor(XR[:, n, LPAD:X_ST], XR[:, n, LPAD:X_ST], IG[:, n % 2, :], ALU.mult)\
                       .then_inc(ix_done, 1)

            def lru_variance(half):
                for m in range(5):
                    dve.wait_ge(decay, 5 * half + m + 1)
                    if 5 * half + m:
                        dve.wait_ge(var_ready, 5 * half + m)
                    own.next(dve.tensor_tensor(tmp[:, 0, :], A5[m], A5[m], ALU.mult))
                    dve.scalar_tensor_tensor(out=R5[:, m, :], in0=tmp[:, 0, :], scalar=1.0, in1=R5[:, m, :],
                                             op0=ALU.add, op1=ALU.mult).then_inc(var_ready, 1)

            def lru_scan(half, m):
                n = 5 * half + m
                xr = XR[:, n, LPAD:X_ST]
                dve.wait_ge(root, n + 1)
                dve.wait_ge(ix_done, n + 1)
                own.next(dve.tensor_tensor(xr, xr, R5[:, m, :], ALU.mult))
                own.next(dve.tensor_tensor_scan(tmp[:, 1, :], A5[m], xr, 0.0, ALU.mult, ALU.add))
                dve.tensor_tensor(RG[:, n, :], tmp[:, 1, :], RG[:, n, :], ALU.mult).then_inc(lru_done, 1)
                dve.wait_ge(lru_done, n + 1)
                dve.tensor_copy(b_hi[:, n, :], RG[:, n, :]).then_inc(b_hi_w, 1)
                dve.wait_ge(b_hi_w, KR + n + 1)
                dve.tensor_tensor(b_lo[:, n, :], RG[:, n, :], b_hi[:, n, :].bitcast(F32), ALU.subtract)\
                   .then_inc(opb, 1)

            def conv_out(half, m):
                if half == 0 and m == 0:
                    dve.wait_ge(ld_ga, 16)
                wait_used(dve, f"convo{half}", 0, 2 * m + 1)
                g = GA[:, 4 * half + m, :]
                dve.scalar_tensor_tensor(out=g, in0=bank_of(f"convo{half}", m)[:, :], scalar=col("conv_b_out", 4 * half + m),
                                         in1=g, op0=ALU.add, op1=ALU.mult).then_inc(evac_of(f"convo{half}", m), 1)

            norm_stat(NORM["ln"])
            for k in range(KD + 1):
                if k < KD:
                    if k > 1:
                        dve.wait_ge(opa, FILL_A["u2"] + k - 1)
                    dve.scalar_tensor_tensor(out=tmp[:, k % 2, :], in0=U[:, k, PAD:U_ST], scalar=col("conv_ln_g", k),
                                             in1=BCAST[:, :], op0=ALU.mult, op1=ALU.mult).then_inc(a_val, 1)
                if k:
                    dve.wait_ge(u_silu, k)
                    dve.tensor_copy(a_hi[:, k - 1, :], tmp[:, (k - 1) % 2, :]).then_inc(a_hi_w, 1)
                    lo_a("u2", k - 1)
                if k in (4, 6):
                    lru_input(0, (k // 2 - 2,))
            filled["a"] = FILL_A["u2"] + KD
            settle()
            lru_input(0, (2, 3, 4))
            lru_variance(0)
            lru_scan(0, 0)
            for m in range(4):
                lru_scan(0, m + 1)
                conv_out(0, m)
            lru_input(1)
            lru_variance(1)
            for m in range(4):
                lru_scan(1, m)
                conv_out(1, m)
            lru_scan(1, 4)
            dve.wait_ge(ld_gb, 16)
            for m in range(KD + 1):
                if m < KD:
                    if m > 1:
                        dve.wait_ge(opa, FILL_A["mix"] + m - 1)
                    wait_used(dve, "lruo", 0, ((m + 1) * KR - 1) // 4)
                    dve.tensor_tensor(tmp[:, m % 2, :], bank_of("lruo", m)[:, :], GB[:, m, :], ALU.mult)\
                       .then_inc(evac_of("lruo", m), 1)
                    wait_evac(dve, "lruo", 0, m)
                    if m == 0:
                        wait_evac(dve, "convo1", 0, 3)
                    dve.tensor_tensor(tmp[:, m % 2, :], tmp[:, m % 2, :], GA[:, m, :], ALU.add).then_inc(a_val, 1)
                if m:
                    lo_a("mix", m - 1)
            filled["a"], filled["b"] = FILL_A["mix"] + KD, FILL_B["yb"] + KR
            dve.wait_ge(ld_x2, 16)
            for m in range(KD):
                wait_used(dve, "mix", 0, 2 * m + 1)
                dve.tensor_tensor(X[:, m, :], X[:, m, :], bank_of("mix", m)[:, :], ALU.add)\
                   .then_inc(evac_of("mix", m), 1)
            norm_stat(NORM["n2"])
            operand_a("hf1", lambda k: col("norm2_g", k))
            ffn(1, True)
            dve.wait_ge(sq_summed, 8 * (NORM["nf"] + 1))
            sums = AUX[:, 0:8].rearrange("p (j w) -> p j w", w=2)
            r1, sum2, r12 = (small[:, r, 0:4] for r in (4, 6, 5))
            rsqrt(sums[:, :, 0], 4, 1.0 / D)
            own.next(dve.tensor_copy(r1, small[:, 1, 0:4]))
            own.next(dve.tensor_tensor(sum2, sums[:, :, 1], r1, ALU.mult))
            own.next(dve.tensor_tensor(sum2, sum2, r1, ALU.mult))
            rsqrt(sum2, 4, 1.0 / D)
            own.next(dve.tensor_tensor(r12, r1, small[:, 1, 0:4], ALU.mult))
            diagonal(small[:, 5, :])
            diagonal(small[:, 4, :], dst=sq[:, 0, :])
            dve.wait_ge(bc_ready, stat[0] - 1)
            operand_a("hf2", lambda k: derived[:, 6, k:k + 1], lambda k: mods[:, k:k + 1])
            dve.wait_ge(bc_ready, stat[0])
            for k in range(KD):
                dve.scalar_tensor_tensor(out=X[:, k, :], in0=X[:, k, :], scalar=col("norm_f_g", k), in1=bank[6][:, :],
                                         op0=ALU.mult, op1=ALU.mult).then_inc(x_ready, 1)
            dve.wait_ge(x_ready, KD)

            def residual(b):
                for k in range(KD + 1):
                    if k < KD:
                        ins = dve.scalar_tensor_tensor(out=Y[:, k, :], in0=Y[:, k, :], scalar=derived[:, 3 + b, k:k + 1],
                                                       in1=BCAST[:, :], op0=ALU.mult, op1=ALU.mult)
                        if k:
                            own.behind(ins)
                        else:
                            own.n += 1
                            ins.then_inc(vchain, 1)
                    else:
                        own.all()
                    if k:
                        dve.tensor_tensor(X[:, k - 1, :], X[:, k - 1, :], Y[:, k - 1, :], ALU.add).then_inc(x_ready, 1)

            def modulated(b, fill):
                operand_a(fill, lambda k: derived[:, b, k:k + 1], lambda k: mods[:, 24 * b + k:24 * b + k + 1])

            ffn(2, False)
            norm_stat(NORM["post1"])
            residual(0)
            norm_stat(NORM["pre2"])
            modulated(1, "hmix2")

            own.next(dve.memset(RESET, 1.0))
            own.next(dve.memset(RESET.rearrange("p (n m) -> p n m", m=P)[:, :, 0:1], 0.0))
            for s, n in ((gla_in, 1), (gla_cp, 1), (fox_out, 2), (fox_t, 2), (fox_o, 2), (fox_pt, 2), (fox_p, 2)):
                dve.memset(small[:, 4, 0:1], 0.0).then_inc(s, n)
                dve.wait_ge(s, n)
            for s, n in ((gla_exp, 1), (gla_mm, 1), (rows_out[0], 16), (rows_out[1], 16)):
                dve.memset(small[:, 4, 0:1], 0.0).then_inc(s, n)
                dve.wait_ge(s, n)
            for h in range(GLA_HEADS):
                dve.wait_ge(la_ln, h + 1)
                own.next(dve.scalar_tensor_tensor(out=LA[:, h, :], in0=LA[:, h, :], scalar=0.0, in1=LT[:, h, :],
                                                  op0=ALU.min, op1=ALU.subtract))
            f_log, f_sum = LOW[32:48, :], LT[32:48, 4, :]
            dve.wait_ge(la_ln, 5)
            own.next(dve.scalar_tensor_tensor(out=f_log, in0=f_log, scalar=0.0, in1=f_sum, op0=ALU.min,
                                              op1=ALU.subtract))
            own.next(dve.tensor_tensor_scan(f_sum, ones[32:48, 0:1].to_broadcast([16, T]), f_log, 0.0, ALU.mult, ALU.add))
            own.next(dve.tensor_scalar(f_log, f_sum, -1.0, None, ALU.mult))
            own.next(dve.tensor_copy(FHL[32:48, :], f_log))
            dve.tensor_tensor(FLO, f_log, FHL[32:48, :].bitcast(F32), ALU.subtract).then_inc(f_split, 1)
            own.next(dve.tensor_copy(ONES_R, ones[:, :]))
            own.next(dve.tensor_tensor(small[32:64, 7, :], ident[32:64, 32:48], ident[32:64, 48:64], ALU.add))

            with dve.Fori(0, GLA_HEADS) as i:
                made, copied = [0], [0]

                def give(label, ins):
                    assert GLA_IN[made[0]] == label, (GLA_IN[made[0]], label)
                    made[0] += 1
                    ins.then_inc(gla_in, 1)
                    dve.wait_ge(gla_in, i * len(GLA_IN) + (made[0] + 1))

                def copy(label, ins):
                    assert GLA_CP[copied[0]] == label, (GLA_CP[copied[0]], label)
                    copied[0] += 1
                    ins.then_inc(gla_cp, 1)
                    dve.wait_ge(gla_cp, i * len(GLA_CP) + (copied[0] + 1))

                def wait_exp(what):
                    dve.wait_ge(gla_exp, i * len(GLA_EXP) + (GLA_EXP.index(what) + 2))

                def wait_mm(what):
                    dve.wait_ge(gla_mm, i * len(GLA_MM) + (GLA_MM.index(what) + 2))

                q_h = QK[:, ds(i * 2, 1), :].rearrange("p a t -> p (a t)")
                k_h = QK[:, ds(i * 2 + 1, 1), :].rearrange("p a t -> p (a t)")

                def blocks(x, l):
                    return x.rearrange("p (n m) -> p n m", m=2 * (P >> l))

                def below(l):
                    m = P >> l
                    b = blocks(BC, l)
                    return dve.tensor_tensor(blocks(E2[l % 2], l), b, b[:, :, m - 1:m].to_broadcast([P, T // (2 * m), 2 * m]),
                                             ALU.subtract)

                def level(l):
                    wait_mm(f"m{l}")
                    dve.memset(small[:, 4, 1:2], 0.0)
                    copy(f"c{l}", dve.copy_predicated(
                        AD.rearrange("p (c t) -> p c t", t=P),
                        masks[:, l:l + 1, :].to_broadcast([P, 4, P]),
                        bank[6 + l % 2][:, :].rearrange("p (c t) -> p c t", t=P)))

                give("bc", dve.tensor_tensor_scan(BC, RESET, LA[:, ds(i, 1), :].rearrange("p a t -> p (a t)"), 0.0,
                                                  ALU.mult, ALU.add))
                give("kc", dve.tensor_copy(KC, k_h))
                copy("ms", dve.memset(AD, 0.0))
                give("d1", below(1))
                level(0)
                give("d2", below(2))
                for l in range(1, 8):
                    m = P >> l
                    wait_exp(f"ef{l}")
                    give(f"k{l}", dve.tensor_tensor(blocks(KQ, l)[:, :, 0:m], blocks(k_h, l)[:, :, 0:m],
                                                    blocks(E2[l % 2], l)[:, :, 0:m], ALU.mult))
                    wait_exp(f"es{l}")
                    give(f"q{l}", dve.tensor_tensor(blocks(KQ, l)[:, :, m:], blocks(q_h, l)[:, :, m:],
                                                    blocks(E2[l % 2], l)[:, :, m:], ALU.mult))
                    if l < 6:
                        give(f"d{l + 2}", below(l + 2))
                    elif l == 6:
                        b = BC.rearrange("p (n m) -> p n m", m=P)
                        give("do", dve.tensor_tensor(E2[0].rearrange("p (n m) -> p n m", m=P),
                                                     b[:, :, P - 1:P].to_broadcast([P, 4, P]), b, ALU.subtract))
                    level(l)
                for n, (at, c) in enumerate(((0, 1), (3, 2), (5, 3))):
                    give(f"x{n}", dve.tensor_tensor(QX[:, at * P:(at + 1) * P], q_h[:, c * P:(c + 1) * P],
                                                    EB[:, c * P:(c + 1) * P], ALU.mult))
                for n, (at, src, c) in enumerate(((4, 5, 2), (1, 3, 1), (2, 4, 1))):
                    give(f"x{n + 3}", dve.tensor_scalar(QX[:, at * P:(at + 1) * P], QX[:, src * P:(src + 1) * P],
                                                        EB[:, (c + 1) * P - 1:(c + 1) * P], None, ALU.mult))
                wait_exp("eo")
                give("kd", dve.tensor_tensor(KQ[:, 0:3 * P], k_h[:, 0:3 * P], E2[0][:, 0:3 * P], ALU.mult))
                wait_mm("o0")
                copy("ao", dve.tensor_copy(AO[:, 0:3 * P], bank[6][:, 0:3 * P]))
                wait_exp("sq3")
                own.begin(i, RSQRT_STEPS)
                rsqrt(small[:, 5, 0:4], 4, 1.0 / GLA_V)
                own.end(GLA_HEADS)
                give("y", dve.tensor_copy(small[:, 6, 0:4], small[:, 1, 0:4]))
                assert made[0] == len(GLA_IN) and copied[0] == len(GLA_CP)

            for t in range(4):
                dve.wait_ge(r_silu, t + 1)
                dve.wait_ge(gla_exp, GLA_HEADS * len(GLA_EXP) + 1)
                for g in range(2):
                    v = ONH[:, 2 * g:2 * g + 2, t, :]
                    dve.tensor_tensor(v, v, R2[:, t, g * SOME:(g + 1) * SOME].rearrange("p (h e) -> p h e", h=2), ALU.mult)\
                       .then_inc(r_prod, 1)
            for j in range(2):
                dve.wait_ge(rows_out[j], 16 * (4 * GLA_HEADS + 1))
            for m in range(KD + 1):
                if m < KD:
                    dve.wait_ge(oa_t, m + 1)
                    if m >= 2:
                        dve.wait_ge(opb, FILL_B["oa"] + m - 1)
                    dve.tensor_scalar(tmp[:, m % 2, :], bank[6 + m % 2][:, :], col("g_gla_2", m), None, ALU.mult)\
                       .then_inc(b_val, 1)
                if m:
                    dve.wait_ge(b_hi_w, FILL_B["oa"] + m)
                    dve.tensor_tensor(b_lo[:, m - 1, :], tmp[:, (m - 1) % 2, :], b_hi[:, m - 1, :].bitcast(F32),
                                      ALU.subtract).then_inc(opb, 1)

            dve.wait_ge(ld_f, 16)
            with dve.Fori(0, FOX_HEADS // 4) as i:
                def forget_sums(h):
                    if h >= 2:
                        dve.wait_ge(fox_s, i * 16 + 4 * (h - 1))
                    dve.tensor_scalar(NFH[32:64, h % 2, :], FHL[32:64, :].bitcast(F32),
                                      small[32:64, 7, ds(i * 4 + h, 1)], None, ALU.mult).then_inc(fox_nf, 1)

                def maximum(u):
                    t = u % 4
                    s_ps = bank[6 + u % 2]
                    dve.wait_ge(fox_s, i * 16 + (u + 1))
                    own.next(dve.tensor_tensor(s_ps[:, t * P:(t + 1) * P], s_ps[:, t * P:(t + 1) * P], tri, ALU.add))
                    own.next(dve.tensor_reduce(small[:, 0, u % 2:u % 2 + 1], s_ps[:, 0:(t + 1) * P], AX_X, ALU.max))
                    dve.tensor_scalar(small[:, 6, t:t + 1], small[:, 0, u % 2:u % 2 + 1], -1.0, None, ALU.mult)\
                       .then_inc(fox_m, 1)

                own.begin(i, 16 * 3)
                forget_sums(0)
                maximum(0)
                maximum(1)
                for u in range(16):
                    h, t = u // 4, u % 4
                    if u < 14:
                        maximum(u + 2)
                    if t == 0 and h < 3:
                        forget_sums(h + 1)
                    dve.wait_ge(fox_o, i * 16 + (u + 3))
                    own.next(dve.reciprocal(small[:, 1, u % 2:u % 2 + 1], small[:, 5, t:t + 1]))
                    dve.tensor_scalar(OB[:, t, ds(i * (4 * FOX_HD) + h * FOX_HD, FOX_HD)],
                                      bank[4 + u % 2][:, 0:FOX_HD], small[:, 1, u % 2:u % 2 + 1], None, ALU.mult)\
                       .then_inc(fox_out, 1)
                own.end(FOX_HEADS // 4)
            for m in range(KD):
                dve.wait_ge(a_hi_w, FILL_A["ob"] + m + 1)
                dve.tensor_tensor(a_lo[:, m, :], bank[6 + m % 2][:, :], a_hi[:, m, :].bitcast(F32), ALU.subtract)\
                   .then_inc(opa, 1)
            for m in range(KD):
                wait_used(dve, "pa", 0, 2 * m + 1)
                dve.wait_ge(gate2, m + 1)
                dve.tensor_tensor(GA2[:, m, :], bank_of("pa", m)[:, :], GA2[:, m, :], ALU.mult)\
                   .then_inc(evac_of("pa", m), 1)
            for m in range(KD + 1):
                if m < KD:
                    wait_used(dve, "pb", 0, 2 * m + 1)
                    dve.wait_ge(gate2, KD + m + 1)
                    dve.wait_ge(opb, FILL_B["merged"] + m - 1)
                    dve.tensor_tensor(tmp[:, m % 2, :], bank_of("pb", m)[:, :], GB2[:, m, :], ALU.mult)\
                       .then_inc(evac_of("pb", m), 1)
                    wait_evac(dve, "pb", 0, m)
                    wait_evac(dve, "pa", 0, m)
                    dve.tensor_tensor(tmp[:, m % 2, :], tmp[:, m % 2, :], GA2[:, m, :], ALU.add).then_inc(b_val, 1)
                if m:
                    dve.wait_ge(b_hi_w, FILL_B["merged"] + m)
                    dve.tensor_tensor(b_lo[:, m - 1, :], tmp[:, (m - 1) % 2, :], b_hi[:, m - 1, :].bitcast(F32),
                                      ALU.subtract).then_inc(opb, 1)
            filled["a"], filled["b"] = FILL_A["ob"] + KD, FILL_B["merged"] + KD
            norm_stat(NORM["post2"])
            residual(1)
            norm_stat(NORM["pre3"])
            modulated(2, "hf3")
            ffn(3, False)
            norm_stat(NORM["post3"])
            residual(2)


def lay_panels(w):
    import numpy as np
    K, N = w.shape
    t = w.reshape(K // P, P, N // P, P).transpose(2, 0, 1, 3).reshape(-1, P, P)
    if t.shape[0] % 4:
        t = np.concatenate([t, np.zeros((4 - t.shape[0] % 4, P, P), t.dtype)])
    return t.reshape(-1, 4, P, P).transpose(0, 2, 1, 3).reshape(-1, P, SOME)


def lay_rows(w):
    K, N = w.shape
    return w.reshape(K // P, P, N // SOME, SOME).transpose(2, 0, 1, 3).reshape(-1, P, SOME)


def lay_wide(w):
    p = lay_panels(w)
    return p.reshape(-1, 4, 2, P, SOME).transpose(0, 2, 1, 3, 4).reshape(-1, P, SOME)


def alternate(a, b):
    import numpy as np
    K, N = a.shape
    return np.stack([a.reshape(K, N // P, P), b.reshape(K, N // P, P)], 2).reshape(K, 2 * N)


def turns(a, b):
    import numpy as np
    return np.stack([a.reshape(-1, 8, P, SOME), b.reshape(-1, 8, P, SOME)], 1).reshape(-1, P, SOME)


def lay_gates(wa, wx, half):
    import numpy as np
    out = []
    for m in range(5 * half, 5 * half + 5):
        for w in (wa, wx):
            full = np.zeros((D_RNN + 2 * P, P), w.dtype)
            for h in range(HEADS_LRU):
                lo, hi = h * LRU_BLOCK, (h + 1) * LRU_BLOCK
                a, b = max(lo, m * P), min(hi, (m + 1) * P)
                if a < b:
                    full[P + lo:P + hi, a - m * P:b - m * P] = w[h][:, a - lo:b - lo]
            blocks = np.concatenate([full[m * P:(m + 3) * P], np.zeros((P, P), w.dtype)]).reshape(4, P, P)
            out.append(blocks.transpose(1, 0, 2).reshape(P, SOME))
    return np.stack(out)


def kernel(**inputs):
    import numpy as np
    import concourse.bacc as bacc
    from concourse.bass_utils import run_bass_kernel_spmd as run

    v = {n: np.asarray(a) for n, a in inputs.items()}
    w_in = v["w_in"][0]
    cuts = [0, D, 2 * D, 2 * D + D_RNN, 2 * D + 2 * D_RNN]
    parts = [lay_wide(alternate(w_in[:, 0:D], w_in[:, D:2 * D])), lay_wide(w_in[:, 2 * D:]),
             lay_gates(v["lru_wa"][0], v["lru_wx"][0], 0), lay_panels(v["conv_w_out"][0][:, :D // 2]),
             lay_gates(v["lru_wa"][0], v["lru_wx"][0], 1), lay_panels(v["conv_w_out"][0][:, D // 2:]),
             lay_panels(v["lru_w_out"][0]), lay_panels(v["w_mix_out"][0])]

    def ffn_panels(g, u, dn):
        a = FA * P
        return [lay_wide(alternate(g[:, :a], u[:, :a])), lay_panels(dn[:a]),
                lay_wide(alternate(g[:, a:], u[:, a:])), lay_panels(dn[a:])]

    parts += ffn_panels(v["ffn_w1"][0], v["ffn_w3"][0], v["ffn_w2"][0])
    parts += ffn_panels(v["w_gu1_2"][0][:, :FF], v["w_gu1_2"][0][:, FF:], v["w_dn1_2"][0])
    w2 = v["w_in_2"][0]
    at = np.cumsum([0, 512, 512, 1024, 16, 1024, 1024, 1024, 1024, 16, 1024, 1024])
    q_a, k_a, v_a, a_low, r_a, q_b, k_b, v_b, f_b, gate_a, gate_b = (w2[:, at[i]:at[i + 1]] for i in range(11))
    low = np.zeros((D, P), w2.dtype)
    low[:, 0:16] = a_low
    low[:, 32:48] = f_b
    parts += [lay_wide(np.concatenate([q_a, k_a], 1)), lay_panels(low), lay_rows(v_a),
              turns(lay_rows(np.concatenate([r_a, v_b], 1)), lay_panels(np.concatenate([gate_a, gate_b], 1))),
              lay_panels(alternate(q_b, k_b)),
              lay_panels(v["w_pa_2"][0]), lay_panels(v["w_pb_2"][0]), lay_panels(v["w_out_2"][0])]
    parts += ffn_panels(v["w_gu2_2"][0][:, :FF], v["w_gu2_2"][0][:, FF:], v["w_dn2_2"][0])
    stream = np.concatenate(parts)[:NPANELS]
    ada = v["w_ada_2"][0].reshape(KD, P, 9, D).transpose(2, 0, 1, 3).reshape(-1, P, D)

    def as_cols(a):
        return a.reshape(-1, P).T

    b_in = v["b_in"][0]
    glu_bias = np.stack([b_in[:D].reshape(-1, P), b_in[D:2 * D].reshape(-1, P)], 1).reshape(-1)
    given = dict(v)
    given["b_in"] = np.concatenate([glu_bias, b_in[2 * D:]])
    columns = []
    for n, (start, count) in COLS.items():
        if n == "b_f_2":
            c = np.zeros((P, 1), np.float32)
            c[32:48, 0] = v[n][0]
        else:
            c = as_cols(given[n])
        assert c.shape == (P, count), (n, c.shape)
        columns.append(c)
    cols = np.concatenate(columns, 1)
    consts = np.stack([np.eye(P, dtype=np.float32), np.triu(np.full((P, P), -1e30, np.float32), 1)], 1)
    s_, t_ = np.arange(P)[:, None], np.arange(P)[None, :]
    masks = [s_ == t_]
    for l in range(1, 8):
        m = P >> l
        masks.append((s_ // (2 * m) == t_ // (2 * m)) & (s_ // m % 2 == 0) & (t_ // m % 2 == 1))
    masks = np.stack(masks, 1).astype(np.float32)

    nc = bacc.Bacc("TRN2", target_bir_lowering=False, num_devices=1)
    arrays = {"stream": stream, "ada": ada, "x": v["x"][0].T.reshape(KD, P, T).transpose(1, 0, 2), "cols": cols,
              "consts": consts, "masks": masks, "wa2": v["w_a2_2"][0]}
    arrays = {n: np.ascontiguousarray(a) for n, a in arrays.items()}
    args = [nc.dram_tensor(f"d_{n}", a.shape, mybir.dt.from_np(a.dtype), kind="ExternalInput").ap() for n, a in arrays.items()]
    args.append(nc.dram_tensor("d_out", (P, KD, T), F32, kind="ExternalOutput").ap())
    args += [nc.dram_tensor(f"spill_{n}", (P, KD, T), F32, kind="Internal").ap() for n in ("ga", "gb")]
    args.append(nc.dram_tensor("spill_rv", (P, 4 * KD, T), F32, kind="Internal").ap())
    build(nc, *args)
    r = run(nc, [{f"d_{n}": a for n, a in arrays.items()}], core_ids=[0])
    y = r.results[0]["d_out"]
    return y.transpose(1, 0, 2).reshape(D, T).T[None]
```
